# Optimizing a Trainium2 kernel written in Bass

```python
import jax, jax.numpy as jnp
from jax import lax
import numpy as np

D_MODEL = 1024
BATCH = 1
SEQ = 128
DEPTH = 1
DEC_BATCH = 1
DEC_SEQ = 512
PAST_LEN = 128

GRID_W = 64
N_FOUR_GROUPS = 4
FOUR_GROUP = 128
FOUR_W = N_FOUR_GROUPS * FOUR_GROUP
N_HEADS = 4
HEAD_K = 128
HEAD_V = 128
HGRN_K_W = N_HEADS * HEAD_K
HGRN_V_W = N_HEADS * HEAD_V
D_FF = 2816
CHUNK = 32
N_MOD = 9
EPS = 1e-6
IN_COLS = FOUR_W + 3 * HGRN_K_W + 2 * HGRN_V_W + 2 * D_MODEL

kernel_name = "hybrid_fnet_hgrn2_macaron_diffusion_step"

def rms_norm(x, gain):
    xf = x.astype(jnp.float32)
    y = xf * lax.rsqrt(jnp.mean(xf * xf, axis=-1, keepdims=True) + EPS)
    return (y * gain.astype(jnp.float32)).astype(x.dtype)

def swiglu(h, w_in, w_out):
    g, u = jnp.split(h @ w_in, 2, axis=-1)
    return (jax.nn.silu(g) * u) @ w_out

def fourier_mix(u, rows):
    B, L, _ = u.shape
    uf = u.astype(jnp.float32)
    if rows is None:
        uf = uf.reshape(B, L, N_FOUR_GROUPS, FOUR_GROUP)
        y = jnp.fft.fftn(uf, axes=(1, 3), norm="ortho").real
    else:
        uf = uf.reshape(B, rows, GRID_W, N_FOUR_GROUPS, FOUR_GROUP)
        y = jnp.fft.fftn(uf, axes=(1, 2, 4), norm="ortho").real
    return y.reshape(B, L, FOUR_W).astype(u.dtype)

def _to_chunks(a):
    B, L, H, E = a.shape
    return a.reshape(B, L // CHUNK, CHUNK, H, E).transpose(1, 0, 3, 2, 4)

def hgrn2_scan(q, f, v, s0):
    B, L, H, _ = q.shape
    log_f = jnp.log(f)
    k = 1.0 - f
    tril = jnp.tril(jnp.ones((CHUNK, CHUNK), dtype=bool))[:, :, None]

    def step(S, inp):
        qc, lfc, kc, vc = inp
        b = jnp.cumsum(lfc, axis=2)
        diff = b[:, :, :, None, :] - b[:, :, None, :, :]
        decay = jnp.where(tril, jnp.exp(jnp.where(tril, diff, 0.0)), 0.0)
        A = jnp.sum(qc[:, :, :, None, :] * kc[:, :, None, :, :] * decay, axis=-1)
        o = (jnp.einsum('bhts,bhsv->bhtv', A, vc)
             + jnp.einsum('bhtk,bhkv->bhtv', qc * jnp.exp(b), S))
        b_last = b[:, :, -1:, :]
        S = (jnp.exp(b_last[:, :, 0, :])[..., None] * S
             + jnp.einsum('bhsk,bhsv->bhkv', kc * jnp.exp(b_last - b), vc))
        return S, o

    s_final, o = lax.scan(step, s0, (_to_chunks(q), _to_chunks(log_f), _to_chunks(k), _to_chunks(v)))
    o = o.transpose(1, 0, 3, 2, 4).reshape(B, L, H, v.shape[-1])
    return o, s_final

def mixer(h, w_in, w_four, hgrn_gain, w_hgrn, w_out, lb, s0_f, s0_b, rows):
    B, L, _ = h.shape
    splits = [int(s) for s in np.cumsum([FOUR_W, HGRN_K_W, HGRN_K_W, HGRN_K_W, HGRN_V_W, HGRN_V_W, D_MODEL])]
    u, q, zf, zb, i, g, ga, gb = jnp.split(h @ w_in, splits, axis=-1)
    branch_a = fourier_mix(u, rows) @ w_four
    qh = jax.nn.silu(q.astype(jnp.float32)).reshape(B, L, N_HEADS, HEAD_K)
    vh = i.astype(jnp.float32).reshape(B, L, N_HEADS, HEAD_V)
    f_f = (lb[0] + (1.0 - lb[0]) * jax.nn.sigmoid(zf.astype(jnp.float32))).reshape(B, L, N_HEADS, HEAD_K)
    f_b = (lb[1] + (1.0 - lb[1]) * jax.nn.sigmoid(zb.astype(jnp.float32))).reshape(B, L, N_HEADS, HEAD_K)
    o_f, s_f = hgrn2_scan(qh, f_f, vh, s0_f)
    o_b, s_b = hgrn2_scan(jnp.flip(qh, 1), jnp.flip(f_b, 1), jnp.flip(vh, 1), s0_b)
    o = o_f + jnp.flip(o_b, 1)
    o = o * lax.rsqrt(jnp.mean(o * o, axis=-1, keepdims=True) + EPS)
    o = o.reshape(B, L, HGRN_V_W) * hgrn_gain.astype(jnp.float32) * jax.nn.silu(g.astype(jnp.float32))
    branch_b = o.astype(h.dtype) @ w_hgrn
    merged = jax.nn.sigmoid(ga) * branch_a + jax.nn.sigmoid(gb) * branch_b
    return merged @ w_out, s_f, s_b

def trunk_layer(x, cond, w_mod, b_mod, norm_pre, norm_post, ffn_w_in, ffn_w_out,
                w_in, w_four, hgrn_gain, w_hgrn, w_out, lb, s0_f, s0_b, rows):
    mod = (jax.nn.silu(cond) @ w_mod + b_mod)[:, None, :]
    sh1, sc1, g1, sh2, sc2, g2, sh3, sc3, g3 = jnp.split(mod, N_MOD, axis=-1)
    h = rms_norm(x, norm_pre[0]) * (1.0 + sc1) + sh1
    x = x + 0.5 * g1 * rms_norm(swiglu(h, ffn_w_in[0], ffn_w_out[0]), norm_post[0])
    h = rms_norm(x, norm_pre[1]) * (1.0 + sc2) + sh2
    m, s_f, s_b = mixer(h, w_in, w_four, hgrn_gain, w_hgrn, w_out, lb, s0_f, s0_b, rows)
    x = x + g2 * rms_norm(m, norm_post[1])
    h = rms_norm(x, norm_pre[2]) * (1.0 + sc3) + sh3
    x = x + 0.5 * g3 * rms_norm(swiglu(h, ffn_w_in[1], ffn_w_out[1]), norm_post[2])
    return x, s_f, s_b

def setup_inputs(seed: int = 0) -> dict:
    key = jax.random.key(seed)
    ks = jax.random.split(key, 17)
    n = jax.random.normal
    f32 = jnp.float32
    return {
        "x_prompt": n(ks[0], (BATCH, SEQ, D_MODEL), f32),
        "x_sample": n(ks[1], (DEC_BATCH, DEC_SEQ, D_MODEL), f32),
        "state_hgrn": 0.5 * n(ks[2], (DEC_BATCH, DEPTH, 2, N_HEADS, HEAD_K, HEAD_V), f32),
        "c": n(ks[3], (DEC_BATCH, D_MODEL), f32),
        "c_ctx": n(ks[4], (D_MODEL,), f32),
        "w_mod": 0.5 * D_MODEL ** -0.5 * n(ks[5], (DEPTH, D_MODEL, N_MOD * D_MODEL), f32),
        "b_mod": 0.01 * n(ks[6], (DEPTH, N_MOD * D_MODEL), f32),
        "norm_pre": 1.0 + 0.05 * n(ks[7], (DEPTH, 3, D_MODEL), f32),
        "norm_post": 1.0 + 0.05 * n(ks[8], (DEPTH, 3, D_MODEL), f32),
        "ffn_w_in": D_MODEL ** -0.5 * n(ks[9], (DEPTH, 2, D_MODEL, 2 * D_FF), f32),
        "ffn_w_out": D_FF ** -0.5 * n(ks[10], (DEPTH, 2, D_FF, D_MODEL), f32),
        "w_in": D_MODEL ** -0.5 * n(ks[11], (DEPTH, D_MODEL, IN_COLS), f32),
        "w_four": FOUR_W ** -0.5 * n(ks[12], (DEPTH, FOUR_W, D_MODEL), f32),
        "hgrn_gain": 1.0 + 0.05 * n(ks[13], (DEPTH, HGRN_V_W), f32),
        "w_hgrn": HGRN_V_W ** -0.5 * n(ks[14], (DEPTH, HGRN_V_W, D_MODEL), f32),
        "w_out": D_MODEL ** -0.5 * n(ks[15], (DEPTH, D_MODEL, D_MODEL), f32),
        "lb_logits": 0.5 * n(ks[16], (DEPTH + 1, 2, HGRN_K_W), f32),
    }

def reference(x_prompt, x_sample, state_hgrn, c, c_ctx, w_mod, b_mod, norm_pre, norm_post,
              ffn_w_in, ffn_w_out, w_in, w_four, hgrn_gain, w_hgrn, w_out, lb_logits):
    lb_all = jnp.cumsum(jax.nn.softmax(lb_logits.astype(jnp.float32), axis=0), axis=0)
    rows = x_sample.shape[1] // GRID_W

    y_prompt = x_prompt
    zero_state = jnp.zeros((x_prompt.shape[0], N_HEADS, HEAD_K, HEAD_V), jnp.float32)
    layer_states = []
    for l in range(DEPTH):
        y_prompt, s_f, s_b = trunk_layer(
            y_prompt, c_ctx[None, :], w_mod[l], b_mod[l], norm_pre[l], norm_post[l],
            ffn_w_in[l], ffn_w_out[l], w_in[l], w_four[l], hgrn_gain[l], w_hgrn[l], w_out[l],
            lb_all[l], zero_state, zero_state, None)
        layer_states.append(jnp.stack([s_f, s_b], axis=1))
    new_state_hgrn = jnp.stack(layer_states, axis=1).astype(x_prompt.dtype)

    y_sample = x_sample
    for l in range(DEPTH):
        y_sample, _, _ = trunk_layer(
            y_sample, c, w_mod[l], b_mod[l], norm_pre[l], norm_post[l],
            ffn_w_in[l], ffn_w_out[l], w_in[l], w_four[l], hgrn_gain[l], w_hgrn[l], w_out[l],
            lb_all[l], state_hgrn[:, l, 0].astype(jnp.float32), state_hgrn[:, l, 1].astype(jnp.float32), rows)

    return (y_prompt, y_sample, new_state_hgrn)


_drawn_inputs = setup_inputs


def setup_inputs(seed=0):
    import zlib

    import numpy as np

    out = dict(_drawn_inputs(seed))
    spreads = {}
    factors = {'state_hgrn': 8.0, 'norm_post': 3.451, 'hgrn_gain': 6.248}
    for name, (base, spread) in spreads.items():
        noise = np.random.default_rng([zlib.crc32(name.encode()), seed]).standard_normal(out[name].shape)
        drawn = base * np.exp(spread * noise) if base else spread * noise
        out[name] = __import__('jax').numpy.asarray(drawn.astype(out[name].dtype))
    for name, factor in factors.items():
        out[name] = (out[name] * factor).astype(out[name].dtype)
    return out
```

```python
import concourse.bass as bass
from concourse import mybir

P = 128
D = 1024
KT = D // P
CTX, LAT = 128, 512
T = CTX + LAT
HALF = T // 2
NCH = T // P
DFF = 2816
FT = DFF // P
NH = 4
NMOD = 9
EPS = 1e-6
TB = T * 4
W_IN_GATES = 3072

fp32 = mybir.dt.float32
fp32r = mybir.dt.float32r
u8 = mybir.dt.uint8
ACT = mybir.ActivationFunctionType
ALU = mybir.AluOpType

PHASES = [
    ("ffn0_in", FT, [1, 1]),
    ("ffn0_out", KT // 2, [1] * 6),
    ("mix_in", 12, [1, 1]),
    ("mix_merge", KT // 2, [1, 1, 2, 1, 1, 2]),
    ("mix_out", KT // 2, [1, 1]),
    ("ffn1_in", FT, [1, 1]),
    ("ffn1_out", KT // 2, [1] * 6),
]
KEYS = [(0, 0), (0, 1), (0, 2), (0, 3), (1, 0), (1, 2), (1, 3), (1, 4)]
OUT_SPLIT = [(0, 8), (8, 7), (15, 7)]


class Phase:

    def __init__(self, slabs, dmas, bodies, kinds):
        self.base, self.raw0, self.bodies, self.kinds = slabs, list(dmas), bodies, kinds
        self.per = len(kinds)
        self.raw_per = [16 * sum(k for n, k in enumerate(kinds) if n % 2 == s) for s in (0, 1)]

    def slab(self, body, pos):
        return body * self.per + (self.base + pos)

    def raw_need(self, body, pos):
        if pos >= self.per:
            body, pos = body + 1, pos - self.per
        s = pos % 2
        within = 16 * sum(k for n, k in enumerate(self.kinds[:pos + 1]) if n % 2 == s)
        return body * self.raw_per[s] + (self.raw0[s] + within)


def plan():
    out, slabs, dmas = {}, 0, [0, 0]
    for name, bodies, kinds in PHASES:
        ph = Phase(slabs, dmas, bodies, kinds)
        out[name] = ph
        slabs += bodies * ph.per
        dmas = [dmas[s] + bodies * ph.raw_per[s] for s in (0, 1)]
    return out, slabs


def hybrid_step_kernel(nc, x_prompt, x_sample, state_hgrn, c, c_ctx, w_mod, b_mod, norm_pre, norm_post,
                       ffn_w_in, ffn_w_out, w_in, w_four, hgrn_gain, w_hgrn, w_out, lb_logits,
                       t_const, t_dft, t_mask, y_prompt, y_sample, new_state):
    PLAN, NSLAB = plan()

    top = [(nc.sbuf_base + 31) // 32 * 32]

    def place(name, shape, dtype, at=None):
        size = mybir.dt.size(dtype)
        for n in shape[1:]:
            size *= n
        if at is None:
            at = top[0]
            top[0] = (at + size + 31) // 32 * 32
        return nc.alloc_sbuf_tensor_at(name, shape, dtype, offset=at)

    XT = place("XT", [P, KT, T], fp32)
    h_at = top[0]
    Hhi = place("Hhi", [P, KT, T], fp32r)
    Hlo = place("Hlo", [P, KT, T], fp32r)
    Y = place("Y", [P, KT, T], fp32, at=h_at)
    mid_at = top[0]
    Mhi = place("Mhi", [P, FT, T], fp32r)
    Mlo = place("Mlo", [P, FT, T], fp32r)
    raw = [place(f"raw{s}", [P, KT, P], fp32) for s in (0, 1)]
    Whi = [place(f"Whi{s}", [P, KT, P], fp32r) for s in (0, 1)]
    Wlo = [place(f"Wlo{s}", [P, KT, P], fp32r) for s in (0, 1)]
    TT = [place(f"TT{s}", [P, T], fp32) for s in (0, 1, 2)]
    ident = place("ident", [P, P + 2], fp32)
    ones_d = place("ones_d", [P, P], fp32)
    ones_h = place("ones_h", [P, P], fp32)
    VA = place("VA", [P, 120], fp32)
    VB = place("VB", [P, 36], fp32)
    MV = place("MV", [P, NMOD * KT, 2], fp32)
    Avec = place("Avec", [P, 3, KT, 2], fp32)
    Gvec = place("Gvec", [P, 3, KT, 2], fp32)
    LB = place("LB", [P, 6, 8], fp32)
    mask = place("mask", [P, 7, P], u8)
    assert top[0] <= nc.sbuf_usable_end, (top[0], nc.sbuf_usable_end)

    def tile_at(n):
        return mid_at + n * TB

    xtok = place("xtok", [P, NCH, D], fp32, at=tile_at(0))
    rowsA = place("rowsA", [120, P], fp32, at=tile_at(8))
    rowsB = place("rowsB", [36, P], fp32, at=tile_at(8) + 512)
    S2 = place("S2", [P, KT, 32], fp32, at=tile_at(8) + 1024)
    modrow = [place(f"modrow{s}", [P, 512], fp32, at=tile_at(9) + 2048 * s) for s in (0, 1)]
    modw = [place(f"modw{s}", [P, KT, 512], fp32, at=tile_at(11) + 16384 * s) for s in range(4)]
    BT = [place(f"BT{s}", [P, T], fp32, at=tile_at(37 + s)) for s in (0, 1)]
    BH = [place(f"BH{s}", [P, T], fp32, at=tile_at(39 + s)) for s in (0, 1)]
    RS = place("RS", [P, T], fp32, at=tile_at(41))
    OUTB = place("OUTB", [P, NCH, D], fp32, at=tile_at(0))
    Yhi = place("Yhi", [P, NH, T], fp32r, at=tile_at(0))
    Ylo = place("Ylo", [P, NH, T], fp32r, at=tile_at(4))
    UT = place("UT", [P, NCH, 512], fp32, at=tile_at(8))
    VRI = place("VRI", [P, 2, NH, T], fp32, at=tile_at(12))
    DFT = place("DFT", [P, 4608], fp32, at=tile_at(20))
    QD = place("QD", [P, 2, NH, T], fp32, at=tile_at(8))
    KD = place("KD", [P, 2, NH, T], fp32, at=tile_at(16))
    FD = place("FD", [P, 2, NH, T], fp32, at=tile_at(24))
    VT = place("VT", [P, NCH, 512], fp32, at=tile_at(32))
    GT = place("GT", [P, NH, T], fp32, at=tile_at(36))
    KTOK = place("KTOK", [P, 8, P], fp32, at=tile_at(40))
    SV = place("SV", [P, 2, 4, P], fp32, at=tile_at(40) + 4096)
    SO = place("SO", [P, 2, P], fp32, at=tile_at(40) + 8192)
    Ohi = place("Ohi", [P, NH, T], fp32r, at=tile_at(8))
    Olo = place("Olo", [P, NH, T], fp32r, at=tile_at(12))
    MGhi = place("MGhi", [P, KT, T], fp32r, at=tile_at(16))
    MGlo = place("MGlo", [P, KT, T], fp32r, at=tile_at(24))

    PP = [nc.alloc_psum_tensor(f"PP{n}", [P, 2, 512], fp32) for n in range(4)]

    def halves(n):
        return PP[n][:, :, 0:HALF]

    def flat(n):
        return PP[n][:, :, :].rearrange("p a b -> p (a b)")

    def two(ap):
        return ap.rearrange("p (a b) -> p a b", a=2)

    sems = {}

    def sem(name):
        if name not in sems:
            sems[name] = nc.alloc_semaphore(name)
        return sems[name]

    raw_full = [sem("raw_full0"), sem("raw_full1")]
    hi_done, lo_done = sem("hi_done"), sem("lo_done")
    slab_done = sem("slab_done")

    TOK = [(0, 0, CTX), (1, CTX, T)]

    KX = [TT[2], place("KX1", [P, T], fp32, at=tile_at(40))]

    maskf = place("maskf", [P, 7, P], fp32, at=tile_at(40))

    def level_ap(tensor, hd, first, tokens, h):
        base = tensor[:, 0, hd, first:first + tokens]
        return bass.AP(base.tensor, base.offset,
                       [[2 * NH * T, P], [2 * h, tokens // (2 * h)], [NH * T + h, 2], [1, h]])

    block_cm = nc.Block()
    block = block_cm.__enter__()

    @block.sync
    def _(sp):
        sp.dma_start(ident[:, :], t_const).then_inc(sem("const_in"), 16)
        sp.dma_start(rowsA[0:72, :], b_mod.rearrange("l (r q) -> (l r) q", q=P)).then_inc(sem("rows_in"), 16)
        sp.dma_start(rowsA[72:96, :], norm_pre.rearrange("l s (r q) -> (l s r) q", q=P)).then_inc(sem("rows_in"), 16)
        sp.dma_start(rowsA[96:120, :], norm_post.rearrange("l s (r q) -> (l s r) q", q=P)).then_inc(sem("rows_in"), 16)
        sp.dma_start(rowsB[0:4, :], hgrn_gain.rearrange("l (r q) -> (l r) q", q=P)).then_inc(sem("rows_in"), 16)
        sp.dma_start(rowsB[4:20, :], lb_logits.rearrange("l d (r q) -> (l d r) q", q=P)).then_inc(sem("rows_in"), 16)
        sp.dma_start(rowsB[20:28, :], c.rearrange("l (r q) -> (l r) q", q=P)).then_inc(sem("rows_in"), 16)
        sp.dma_start(rowsB[28:36, :], c_ctx.rearrange("(r q) -> r q", q=P)).then_inc(sem("rows_in"), 16)
        sp.dma_start(xtok[:, 0, :], x_prompt[0]).then_inc(sem("x_in"), 16)
        sp.dma_start(xtok[:, 1:NCH, :], x_sample[0].rearrange("(a p) f -> p a f", p=P)).then_inc(sem("x_in"), 16)
        wm = w_mod[0].rearrange("(k p) n -> p k n", p=P)
        for i in range(4):
            sp.dma_start(modw[i][:, :, :], wm[:, :, i * 512:(i + 1) * 512]).then_inc(sem(f"modw_in{i}"), 16)
        for i in range(4, 18):
            sp.wait_ge(sem("mod_mm"), i - 3)
            sp.dma_start(modw[i % 4][:, :, :], wm[:, :, i * 512:(i + 1) * 512]).then_inc(sem(f"modw_in{i % 4}"), 16)

        def load(ph, body, pos, parts, first=False):
            if not first:
                sp.wait_ge(lo_done, ph.slab(body, pos) - 1)
            for k0, kn, src in parts:
                sp.dma_start(raw[pos % 2][:, k0:k0 + kn, :], src).then_inc(raw_full[pos % 2], 16)

        def col(ap, start):
            return ap[:, :, bass.ds(start, P)]

        def load_ffn_in(f):
            ph = PLAN[f"ffn{f}_in"]
            w = ffn_w_in[0, f].rearrange("(k p) n -> p k n", p=P)
            if f == 0:
                load(ph, 0, 0, [(0, KT, w[:, :, 0:P])], first=True)
                load(ph, 0, 1, [(0, KT, w[:, :, DFF:DFF + P])], first=True)
            else:
                load(ph, 0, 0, [(0, KT, w[:, :, 0:P])])
                load(ph, 0, 1, [(0, KT, w[:, :, DFF:DFF + P])])
            with sp.Fori(1, FT) as j:
                load(ph, j, 0, [(0, KT, col(w, j * P))])
                load(ph, j, 1, [(0, KT, col(w, j * P + DFF))])

        def load_ffn_out(f):
            ph = PLAN[f"ffn{f}_out"]
            w = ffn_w_out[0, f].rearrange("(k p) n -> p k n", p=P)
            with sp.Fori(0, ph.bodies) as j:
                for n2 in range(2):
                    for s, (k0, kn) in enumerate(OUT_SPLIT):
                        load(ph, j, 3 * n2 + s, [(0, kn, w[:, k0:k0 + kn, bass.ds(j * 2 * P + n2 * P, P)])])

        load_ffn_in(0)
        load_ffn_out(0)
        wi = w_in[0].rearrange("(k p) n -> p k n", p=P)
        ph = PLAN["mix_in"]
        with sp.Fori(0, ph.bodies) as j:
            for s in range(2):
                load(ph, j, s, [(0, KT, col(wi, j * 2 * P + s * P))])
        ph = PLAN["mix_merge"]
        w4 = w_four[0].rearrange("(k p) n -> p k n", p=P)
        wh = w_hgrn[0].rearrange("(k p) n -> p k n", p=P)
        with sp.Fori(0, ph.bodies) as j:
            for n2 in range(2):
                at = j * 2 * P + n2 * P
                load(ph, j, 3 * n2, [(0, KT, col(wi, at + W_IN_GATES))])
                load(ph, j, 3 * n2 + 1, [(0, KT, col(wi, at + (W_IN_GATES + D)))])
                load(ph, j, 3 * n2 + 2, [(0, NH, col(w4, (j * P + n2 * (P // 2)) * 2)), (NH, NH, col(wh, at))])
        ph = PLAN["mix_out"]
        wo = w_out[0].rearrange("(k p) n -> p k n", p=P)
        with sp.Fori(0, ph.bodies) as j:
            for s in range(2):
                load(ph, j, s, [(0, KT, col(wo, j * 2 * P + s * P))])
        load_ffn_in(1)
        load_ffn_out(1)
        for part in range(2):
            sp.wait_ge(sem("out_tile"), 4 * (part + 1))
            cols = slice(512 * part, 512 * (part + 1))
            sp.dma_start(y_prompt[0][:, cols], OUTB[:, 0, cols]).then_inc(sem("y_out"), 16)
            sp.dma_start(y_sample[0].rearrange("(a p) f -> p a f", p=P)[:, :, cols],
                         OUTB[:, 1:NCH, cols]).then_inc(sem("y_out"), 16)
        sp.wait_ge(sem("y_out"), 64)

    @block.gpsimd
    def _(pool):
        pool.wait_ge(slab_done, PLAN["mix_in"].base)
        pool.dma_start(DFT[:, :], t_dft).then_inc(sem("dft_in"), 16)
        pool.wait_ge(sem("h_ready"), 2 * KT)
        pool.dma_start(maskf[:, :, :], t_mask).then_inc(sem("mask_in"), 16)
        for hd in range(NH):
            if hd:
                pool.wait_ge(sem("o_mm"), hd)
            for d in range(2):
                pool.dma_start(SV[:, d, 0, :], state_hgrn[0, 0, d, hd]).then_inc(sem("state_in"), 16)
            pool.wait_ge(sem("so_ready"), hd + 1)
            for d in range(2):
                pool.dma_start(new_state[0, 0, d, hd], SO[:, d, :]).then_inc(sem("state_out"), 16)
        pool.wait_ge(sem("state_out"), 16 * 2 * NH)

    @block.tensor
    def _(pe):
        mm = nc.tensor.matmul

        def slab(ph, body, pos, rhs, outs, k_total=KT, first_slab=True, last_slab=True):
            pe.wait_ge(lo_done, ph.slab(body, pos) + 1)
            s = pos % 2
            count = {}
            last = None
            for k, ((hi, lo), out) in enumerate(zip(rhs, outs)):
                n = outs.count(out)
                seen = count.get(out, 0)
                count[out] = seen + 1
                for a, (w, x) in enumerate(((Whi[s], hi), (Whi[s], lo), (Wlo[s], hi))):
                    for half in range(2):
                        last = mm(PP[out][:, half, 0:HALF], w[:, k, :], x[:, half * HALF:(half + 1) * HALF],
                                  start=first_slab and seen == 0 and a == 0,
                                  stop=last_slab and seen == n - 1 and a == 2)
            last.then_inc(slab_done, 1)

        h_tiles = [(Hhi[:, k, :], Hlo[:, k, :]) for k in range(KT)]

        def stat(src, n, out, one, first=True, last=True):
            for half in range(2):
                m = mm(PP[out][:, half, 0:HALF], one[:, :], src[:, half * HALF:(half + 1) * HALF],
                       start=first, stop=last)
            return m

        def transpose(out, in_):
            k = in_.shape[0]
            return nc.tensor.transpose(out, in_, ident[0:k, 0:k])

        pe.wait_ge(sem("const_in"), 16)
        pe.wait_ge(sem("rows_in"), 16 * 7)
        transpose(PP[2][:, 0, 0:120], rowsA[:, :]).then_inc(sem("vec_T"), 1)
        transpose(PP[2][:, 1, 0:36], rowsB[:, :]).then_inc(sem("vec_T"), 1)
        pe.wait_ge(sem("x_in"), 32)
        pe.wait_ge(sem("ones_set"), 2)
        for n in range(KT):
            if n >= 2:
                pe.wait_ge(sem("x_sq"), n - 1)
            for ch in range(NCH):
                m = transpose(flat(n % 2)[:, ch * P:(ch + 1) * P], xtok[:, ch, n * P:(n + 1) * P])
            m.then_inc(sem("x_T"), 1)
            if n >= 1:
                pe.wait_ge(sem("x_sq"), n)
                stat(TT[(n - 1) % 2], n - 1, 3, ones_d, n == 1, False).then_inc(sem("x_stat"), 1)
        pe.wait_ge(sem("x_sq"), KT)
        stat(TT[(KT - 1) % 2], KT - 1, 3, ones_d, False, True).then_inc(sem("x_stat"), 1)
        pe.wait_ge(sem("silu_c"), 2)

        def fold_mod(i):
            pe.wait_ge(sem("modrow"), i + 1)
            for q in range(4):
                m = mm(PP[2][:, 0, 2 * (4 * i + q):2 * (4 * i + q) + 2], modrow[i % 2][:, q * P:(q + 1) * P],
                       ident[:, P:P + 2], start=True, stop=True)
            m.then_inc(sem("mod_fold"), 1)

        for i in range(18):
            pe.wait_ge(sem(f"modw_in{i % 4}"), 16 * (i // 4 + 1))
            if i >= 2:
                pe.wait_ge(sem("modrow"), i - 1)
            for k in range(KT):
                q = k % 4
                m = mm(PP[i % 2][32 * q:32 * q + 32, 0, :], S2[:, k, :], modw[i % 4][:, k, :],
                       start=k < 4, stop=k >= 4)
            m.then_inc(sem("mod_mm"), 1)
            if i >= 1:
                fold_mod(i - 1)
        fold_mod(17)

        def ffn_in(f):
            ph = PLAN[f"ffn{f}_in"]
            with pe.Fori(0, FT) as j:
                pe.wait_ge(sem("gate_ready"), j + (f * FT + 1))
                slab(ph, j, 0, h_tiles, [0] * KT)
                pe.wait_ge(sem("hid_ready"), j + (f * FT + 1))
                slab(ph, j, 1, h_tiles, [1] * KT)

        def ffn_out(f, y0):
            ph = PLAN[f"ffn{f}_out"]
            with pe.Fori(0, ph.bodies) as j:
                for n2 in range(2):
                    pe.wait_ge(sem("y_sq"), j * 2 + (y0 + n2 + 1))
                    for s, (k0, kn) in enumerate(OUT_SPLIT):
                        pe.wait_ge(sem("mid_lo"), f * FT + k0 + kn + 1)
                        slab(ph, j, 3 * n2 + s, [(Mhi[:, k, :], Mlo[:, k, :]) for k in range(k0, k0 + kn)],
                             [n2] * kn, first_slab=s == 0, last_slab=s == 2)

        def boundary(b, y0, last=False):
            pe.wait_ge(sem("acc_done"), y0 + KT + 2)
            stat(TT[2], 0, 2, ones_d).then_inc(sem("y_stat"), 1)
            if last:
                for n in range(KT):
                    pe.wait_ge(sem("x_new"), b * KT + n + 1)
                    if n >= 2:
                        pe.wait_ge(sem("out_tile"), n - 1)
                    for ch in range(NCH):
                        m = transpose(flat(n % 2)[:, ch * P:(ch + 1) * P], XT[:, n, ch * P:(ch + 1) * P])
                    m.then_inc(sem("out_T"), 1)
                return
            for n in range(KT):
                pe.wait_ge(sem("x_sq"), (b + 1) * KT + n + 1)
                stat(TT[n % 2], n, 3, ones_d, n == 0, n == KT - 1).then_inc(sem("x_stat"), 1)

        pe.wait_ge(sem("h_ready"), KT)
        ffn_in(0)
        ffn_out(0, 0)
        boundary(0, 0)

        pe.wait_ge(sem("h_ready"), 2 * KT)
        ph = PLAN["mix_in"]

        def plain(first, bodies):
            with pe.Fori(first, first + bodies) as j:
                for s in range(2):
                    pe.wait_ge(sem("t_free"), j * 2 + (s + 1))
                    slab(ph, j, s, h_tiles, [s] * KT)

        def transposed(first, bodies, k0):
            with pe.Fori(0, bodies) as b:
                j = b + first
                for s in range(2):
                    pe.wait_ge(sem("t_free"), j * 2 + (s + 1))
                    slab(ph, j, s, h_tiles, [s] * KT)
                for s in range(2):
                    pe.wait_ge(sem("t_ready"), j * 2 + (s + 1))
                    for ch in range(NCH):
                        m = transpose(flat(2 + s)[:, ch * P:(ch + 1) * P], TT[s][:, ch * P:(ch + 1) * P])
                    m.then_inc(sem("tok_T"), 1)

        transposed(0, 2, 0)
        pe.wait_ge(sem("dft_in"), 16)
        pe.wait_ge(sem("t_free"), 4 + 2)

        def pos_dft(g):
            if g >= 2:
                pe.wait_ge(sem("v_re"), g - 1)
                pe.wait_ge(sem("v_im"), g - 1)
            pr, bank = 2 * (g % 2), g % 2
            u = lambda ch: UT[:, ch, g * P:(g + 1) * P]
            mm(PP[pr][:, 0, 0:P], u(0), DFT[:, 256:384], start=True, stop=True)
            mm(PP[pr][:, 0, P:2 * P], u(0), DFT[:, 384:512], start=True, stop=True)
            for part, out in ((0, PP[pr][:, 1, :]), (1, PP[1][:, bank, :])):
                for a in range(4):
                    at = 512 + part * 2048 + a * 512
                    m = mm(out, u(1 + a), DFT[:, at:at + 512], start=a == 0, stop=a == 3)
            m.then_inc(sem("v_ready"), 1)

        def ch_dft(g):
            pe.wait_ge(sem("v_re"), g + 1)
            pe.wait_ge(sem("v_im"), g + 1)
            if g:
                pe.wait_ge(sem("ylo_done"), g)
            for half in range(2):
                cols = slice(half * HALF, (half + 1) * HALF)
                mm(PP[3][:, half, 0:HALF], DFT[:, 0:P], VRI[:, 0, g, cols], start=True, stop=False)
                m = mm(PP[3][:, half, 0:HALF], DFT[:, P:2 * P], VRI[:, 1, g, cols], start=False, stop=True)
            m.then_inc(sem("yf_ready"), 1)

        pos_dft(0)
        pos_dft(1)
        ch_dft(0)
        pos_dft(2)
        ch_dft(1)
        pos_dft(3)
        ch_dft(2)
        ch_dft(3)
        plain(2, 6)
        pe.wait_ge(sem("ylo_done"), 4)
        transposed(8, 2, 4)
        plain(10, 2)
        pe.wait_ge(sem("t_free"), 24 + 2)

        for hp in range(NH // 2):
            heads = (2 * hp, 2 * hp + 1)
            for lev in range(8):
                for a, hd in enumerate(heads):
                    if lev:
                        pe.wait_ge(sem("kx_ready"), 14 * hp + 2 * (lev - 1) + a + 1)
                    if lev == 1:
                        pe.wait_ge(sem("at_start"), 2 * hp + a + 1)
                    elif lev > 1:
                        pe.wait_ge(sem("at_done"), 14 * hp + 2 * (lev - 2) + a + 1)
                    for ch in range(NCH):
                        out = flat(a)[:, ch * P:(ch + 1) * P]
                        if lev == 0:
                            q = QD[:, 0, hd, ch * P:(ch + 1) * P]
                            mm(out, KD[:, 0, hd, ch * P:(ch + 1) * P], q, start=True, stop=False)
                            m = mm(out, KD[:, 1, hd, ch * P:(ch + 1) * P], q, start=False, stop=True)
                        else:
                            h = 1 << (lev - 1)
                            m = mm(out, KX[a][:, ch * P:(ch + 1) * P], level_ap(QD, hd, ch * P, P, h),
                                   start=True, stop=True)
                    m.then_inc(sem("lev_mm"), 1)
            for a, hd in enumerate(heads):
                pe.wait_ge(sem("upd_done"), 16 * hp + 14 + a + 1)
                if hd:
                    pe.wait_ge(sem("ktok"), hd)
                for e, (d, ch) in enumerate(KEYS):
                    m = transpose(flat(2)[:, e * P:(e + 1) * P], KD[:, d, hd, ch * P:(ch + 1) * P])
                m.then_inc(sem("kT"), 1)
                pe.wait_ge(sem("ktok"), hd + 1)
                if hd:
                    pe.wait_ge(sem("sv_done"), hd)
                for e, (d, ch) in enumerate(KEYS):
                    m = mm(flat(3)[:, e * P:(e + 1) * P], KTOK[:, e, :], VT[:, ch, hd * P:(hd + 1) * P],
                           start=True, stop=True)
                m.then_inc(sem("kv_mm"), 1)
                pe.wait_ge(sem("sv_done"), hd + 1)
                pe.wait_ge(sem("at_done"), 14 * hp + 12 + a + 1)
                for ch in range(NCH):
                    out = flat(a)[:, ch * P:(ch + 1) * P]
                    m = mm(out, VT[:, ch, hd * P:(hd + 1) * P], TT[a][:, ch * P:(ch + 1) * P],
                           start=True, stop=ch == 0)
                    if ch:
                        mm(out, SV[:, 0, ch - 1, :], QD[:, 1, hd, ch * P:(ch + 1) * P], start=False, stop=False)
                        m = mm(out, SV[:, 1, 4 - ch, :], QD[:, 0, hd, ch * P:(ch + 1) * P], start=False, stop=True)
                m.then_inc(sem("o_mm"), 1)
                pe.wait_ge(sem("o_sq"), hd + 1)
                stat(TT[2], 0, 2, ones_h).then_inc(sem("o_stat"), 1)
                pe.wait_ge(sem("o_done"), hd + 1)

        ph = PLAN["mix_merge"]
        fh = [(Yhi[:, k, :], Ylo[:, k, :]) for k in range(NH)] + [(Ohi[:, k, :], Olo[:, k, :]) for k in range(NH)]
        with pe.Fori(0, ph.bodies) as j:
            for n2 in range(2):
                pe.wait_ge(sem("ga_ready"), j * 2 + (n2 + 1))
                slab(ph, j, 3 * n2, h_tiles, [0] * KT)
                pe.wait_ge(sem("gb_ready"), j * 2 + (n2 + 1))
                slab(ph, j, 3 * n2 + 1, h_tiles, [1] * KT)
                pe.wait_ge(sem("branch_b"), j * 2 + (n2 + 1))
                slab(ph, j, 3 * n2 + 2, fh, [2] * NH + [3] * NH)
        pe.wait_ge(sem("mg_done"), KT + 1)
        ph = PLAN["mix_out"]
        mg = [(MGhi[:, k, :], MGlo[:, k, :]) for k in range(KT)]
        with pe.Fori(0, ph.bodies) as j:
            for s in range(2):
                pe.wait_ge(sem("y_sq"), j * 2 + (KT + s + 1))
                slab(ph, j, s, mg, [s] * KT)
        boundary(1, KT)
        pe.wait_ge(sem("h_ready"), 3 * KT)
        ffn_in(1)
        ffn_out(1, 2 * KT)
        boundary(2, 2 * KT, last=True)

    @block.scalar
    def _(act):
        A = nc.scalar.activation

        def split_hi(ph, body, pos):
            act.wait_ge(raw_full[pos % 2], ph.raw_need(body, pos + 2))
            A(Whi[pos % 2][:, :, :], raw[pos % 2][:, :, :], ACT.Copy).then_inc(hi_done, 1)

        def slab_wait(ph, body, pos):
            act.wait_ge(slab_done, ph.slab(body, pos) + 1)

        act.wait_ge(sem("vec_T"), 2)
        act.wait_ge(sem("s2_zero"), 1)
        A(VA[:, :], PP[2][:, 0, 0:120], ACT.Copy).then_inc(sem("vec_evac"), 1)
        A(VB[:, :], PP[2][:, 1, 0:36], ACT.Copy).then_inc(sem("vec_evac"), 1)
        A(TT[2][:, 1:2], PP[2][:, 0, 0:1], ACT.Copy).then_inc(sem("gate_ready"), 1)
        A(TT[2][:, 2:3], PP[2][:, 0, 0:1], ACT.Copy).then_inc(sem("mid_hi"), 1)
        A(TT[2][:, 3:4], PP[2][:, 0, 0:1], ACT.Copy).then_inc(sem("ga_ready"), 1)
        A(TT[2][:, 4:5], PP[2][:, 0, 0:1], ACT.Copy).then_inc(sem("gb_ready"), 1)
        A(TT[2][:, 5:6], PP[2][:, 0, 0:1], ACT.Copy).then_inc(sem("y_sq"), 2)
        A(S2[:, :, 0], PP[2][:, 1, 28:36], ACT.Silu).then_inc(sem("silu_c"), 1)
        A(S2[:, :, 1], PP[2][:, 1, 20:28], ACT.Silu).then_inc(sem("silu_c"), 1)
        act.wait_ge(sem("lb_max"), 1)
        A(LB[:, 2:4, :], LB[:, 2:4, :], ACT.Exp).then_inc(sem("lb_exp"), 1)
        for n in range(KT):
            act.wait_ge(sem("x_T"), n + 1)
            A(XT[:, n, :], flat(n % 2)[:, 0:T], ACT.Copy)
            if n >= 2:
                act.wait_ge(sem("x_stat"), n - 1)
            A(TT[n % 2][:, :], flat(n % 2)[:, 0:T], ACT.Square).then_inc(sem("x_sq"), 1)
        for i in range(18):
            act.wait_ge(sem("mod_mm"), i + 1)
            if i >= 2:
                act.wait_ge(sem("mod_fold"), i - 1)
            A(modrow[i % 2][:, :], PP[i % 2][:, 0, :], ACT.Copy).then_inc(sem("modrow"), 1)
        ph = PLAN["ffn0_in"]
        for s in range(2):
            act.wait_ge(raw_full[s], 16)
            A(Whi[s][:, :, :], raw[s][:, :, :], ACT.Copy).then_inc(hi_done, 1)

        def make_h(b):
            act.wait_ge(sem("x_stat"), (b + 1) * KT)
            A(RS[:, :].rearrange("p (a b) -> p a b", a=2), halves(3), ACT.Sqrt, bias=EPS).then_inc(sem("x_std"), 1)
            for n in range(KT):
                act.wait_ge(sem("h_scaled"), b * KT + n + 1)
                if n >= 2:
                    act.wait_ge(sem("h_ready"), b * KT + n - 1)
                for cond, t0, t1 in TOK:
                    m = A(BH[n % 2][:, t0:t1], BT[n % 2][:, t0:t1], ACT.Identity,
                          bias=MV[:, 3 * b * KT + n, cond:cond + 1], scale=Avec[:, b, n, cond:cond + 1])
                m.then_inc(sem("h_full"), 1)
                act.wait_ge(sem("h_full"), b * KT + n + 1)
                A(Hhi[:, n, :], BH[n % 2][:, :], ACT.Copy).then_inc(sem("h_hi"), 1)

        def boundary(b, last=False):
            act.wait_ge(sem("y_stat"), b + 1)
            A(RS[:, :].rearrange("p (a b) -> p a b", a=2), halves(2), ACT.Sqrt, bias=EPS).then_inc(sem("y_std"), 1)
            for n in range(KT):
                if last:
                    act.wait_ge(sem("out_T"), n + 1)
                    A(OUTB[:, :, n * P:(n + 1) * P], flat(n % 2)[:, 0:T].rearrange("p (a b) -> p a b", a=NCH),
                      ACT.Copy).then_inc(sem("out_tile"), 1)
                else:
                    act.wait_ge(sem("x_new"), b * KT + n + 1)
                    if n >= 2:
                        act.wait_ge(sem("x_stat"), (b + 1) * KT + n - 1)
                    A(TT[n % 2][:, :], XT[:, n, :], ACT.Square).then_inc(sem("x_sq"), 1)

        def ffn_in(f):
            ph = PLAN[f"ffn{f}_in"]
            with act.Fori(0, FT) as j:
                slab_wait(ph, j, 0)
                act.wait_ge(sem("hid_ready"), j + (f * FT + 1))
                A(two(TT[0][:, :]), halves(0), ACT.Silu).then_inc(sem("gate_ready"), 1)
                split_hi(ph, j, 0)
                slab_wait(ph, j, 1)
                split_hi(ph, j, 1)
                act.wait_ge(sem("hid_ready"), j + (f * FT + 2))
                A(Mhi[:, bass.ds(j, 1), :], TT[1][:, :].rearrange("p (a b) -> p a b", a=1), ACT.Copy)\
                    .then_inc(sem("mid_hi"), 1)

        def evac_y(j, n2, y0):
            act.wait_ge(sem("acc_done"), j * 2 + (y0 + n2 + 1))
            A(Y[:, bass.ds(j * 2 + n2, 1), :].rearrange("p a (b c) -> p (a b) c", b=2), halves(n2), ACT.Copy)
            A(two(TT[n2][:, :]), halves(n2), ACT.Square).then_inc(sem("y_sq"), 1)

        def ffn_out(f, y0, last=False):
            ph = PLAN[f"ffn{f}_out"]
            bodies = ph.bodies - 1 if last else ph.bodies
            with act.Fori(0, bodies) as j:
                for n2 in range(2):
                    for s in range(3):
                        slab_wait(ph, j, 3 * n2 + s)
                        split_hi(ph, j, 3 * n2 + s)
                    evac_y(j, n2, y0)
            if last:
                for n2 in range(2):
                    for s in range(3):
                        slab_wait(ph, bodies, 3 * n2 + s)
                        if 3 * n2 + s < 4:
                            split_hi(ph, bodies, 3 * n2 + s)
                    evac_y(bodies, n2, y0)

        make_h(0)
        ffn_in(0)
        ffn_out(0, 0)
        boundary(0)
        make_h(1)

        def fourier_re(g):
            act.wait_ge(sem("v_ready"), g + 1)
            pr = 2 * (g % 2)
            A(VRI[:, :, g, 0:P], PP[pr][:, 0, 0:2 * P].rearrange("p (a b) -> p a b", a=2), ACT.Copy)
            A(VRI[:, 0, g, P:T], PP[pr][:, 1, :], ACT.Copy).then_inc(sem("v_re"), 1)

        def fourier_hi(g):
            act.wait_ge(sem("yf_ready"), g + 1)
            A(two(Yhi[:, g, :]), halves(3), ACT.Copy).then_inc(sem("yhi_done"), 1)

        ph = PLAN["mix_in"]
        for i in range(24):
            s, section = i % 2, i // NH
            slab_wait(ph, i // 2, s)
            act.wait_ge(sem("t_free"), i + 1)
            func = ACT.Copy if section in (0, 4) else ACT.Sigmoid
            A(two(TT[s][:, :]), halves(s), func).then_inc(sem("t_ready"), 1)
            split_hi(ph, i // 2, s)
            if i == 3:
                for g in range(NH):
                    fourier_re(g)
                    if g >= 1:
                        fourier_hi(g - 1)
                fourier_hi(NH - 1)

        for hp in range(NH // 2):
            for a in range(2):
                act.wait_ge(sem("lev_mm"), 16 * hp + a + 1)
                A(TT[a][:, :], flat(a)[:, 0:T], ACT.Copy).then_inc(sem("at_start"), 1)
            act.wait_ge(sem("mask_set"), 1)
            for lev in range(1, 8):
                h = 1 << (lev - 1)
                for a in range(2):
                    act.wait_ge(sem("upd_done"), 16 * hp + 2 * (lev - 1) + a + 1)
                    if lev > 1:
                        act.wait_ge(sem("lev_mm"), 16 * hp + 2 * (lev - 1) + a + 1)
                    A(KX[a][:, :].rearrange("p (b e c) -> p b e c", e=2, c=h), level_ap(KD, 2 * hp + a, 0, T, h),
                      ACT.Copy).then_inc(sem("kx_ready"), 1)
            for a in range(2):
                hd = 2 * hp + a
                act.wait_ge(sem("kT"), hd + 1)
                for bank in range(2):
                    m = A(KTOK[:, 4 * bank:4 * bank + 4, :], PP[2][:, bank, :].rearrange("p (a b) -> p a b", a=4),
                          ACT.Copy)
                m.then_inc(sem("ktok"), 1)
                act.wait_ge(sem("kv_mm"), hd + 1)
                if hd:
                    act.wait_ge(sem("state_out"), 32 * hd)
                A(SO[:, 0, :], PP[3][:, 0, 0:P], ACT.Copy)
                A(SO[:, 1, :], PP[3][:, 1, 0:P], ACT.Copy).then_inc(sem("so_ready"), 1)
                act.wait_ge(sem("o_mm"), hd + 1)
                A(TT[2][:, :], flat(a)[:, 0:T], ACT.Square).then_inc(sem("o_sq"), 1)
                act.wait_ge(sem("o_stat"), hd + 1)
                A(two(TT[2][:, :]), halves(2), ACT.Sqrt, bias=EPS).then_inc(sem("o_std"), 1)
                act.wait_ge(sem("o_full"), hd + 1)
                A(Ohi[:, hd, :], TT[2][:, :], ACT.Copy).then_inc(sem("o_hi"), 1)

        ph = PLAN["mix_merge"]
        with act.Fori(0, ph.bodies) as j:
            for n2 in range(2):
                slab_wait(ph, j, 3 * n2)
                act.wait_ge(sem("mg_ready"), j * 2 + (n2 + 1))
                A(two(TT[0][:, :]), halves(0), ACT.Sigmoid).then_inc(sem("ga_ready"), 1)
                split_hi(ph, j, 3 * n2)
                slab_wait(ph, j, 3 * n2 + 1)
                A(two(TT[1][:, :]), halves(1), ACT.Sigmoid).then_inc(sem("gb_ready"), 1)
                split_hi(ph, j, 3 * n2 + 1)
                slab_wait(ph, j, 3 * n2 + 2)
                split_hi(ph, j, 3 * n2 + 2)
                act.wait_ge(sem("mg_ready"), j * 2 + (n2 + 2))
                A(MGhi[:, bass.ds(j * 2 + n2, 1), :], TT[2][:, :].rearrange("p (a b) -> p a b", a=1), ACT.Copy)\
                    .then_inc(sem("mg_hi"), 1)
        ph = PLAN["mix_out"]
        with act.Fori(0, ph.bodies) as j:
            for s in range(2):
                slab_wait(ph, j, s)
                split_hi(ph, j, s)
                evac_y(j, s, KT)
        boundary(1)
        make_h(2)
        ffn_in(1)
        ffn_out(1, 2 * KT, last=True)
        boundary(2, last=True)

    @block.vector
    def _(dve):
        V = nc.vector

        def split_lo(ph, body, pos):
            dve.wait_ge(hi_done, ph.slab(body, pos) + 3)
            s = pos % 2
            V.tensor_tensor(Wlo[s][:, :, :], raw[s][:, :, :], Whi[s][:, :, :].bitcast(fp32), ALU.subtract)\
                .then_inc(lo_done, 1)

        chain = [0]

        def link(ins):
            chain[0] += 1
            ins.then_inc(sem("dve_chain"), 1)
            dve.wait_ge(sem("dve_chain"), chain[0])

        V.memset(S2[:, :, :], 0.0).then_inc(sem("s2_zero"), 1)
        V.memset(ones_d[:, :], 1.0 / D).then_inc(sem("ones_set"), 1)
        V.memset(ones_h[:, :], 1.0 / P).then_inc(sem("ones_set"), 1)
        V.memset(LB[:, 0, 1:2], 0.0).then_inc(sem("hid_ready"), 1)
        V.memset(LB[:, 0, 6:7], 0.0).then_inc(sem("mid_lo"), 1)
        V.memset(LB[:, 0, 7:8], 0.0).then_inc(sem("mg_done"), 1)
        V.memset(LB[:, 0, 2:3], 0.0).then_inc(sem("mg_ready"), 1)
        V.memset(LB[:, 0, 3:4], 0.0).then_inc(sem("branch_b"), 1)
        V.memset(LB[:, 0, 4:5], 0.0).then_inc(sem("t_free"), 2)
        V.memset(LB[:, 0, 5:6], 0.0).then_inc(sem("acc_done"), 2)
        dve.wait_ge(sem("vec_evac"), 2)
        link(V.tensor_tensor(LB[:, 1, :], VB[:, 4:12], VB[:, 12:20], ALU.max))
        link(V.tensor_tensor(LB[:, 2, :], VB[:, 4:12], LB[:, 1, :], ALU.subtract))
        V.tensor_tensor(LB[:, 3, :], VB[:, 12:20], LB[:, 1, :], ALU.subtract).then_inc(sem("lb_max"), 1)
        dve.wait_ge(sem("lb_exp"), 1)
        link(V.tensor_tensor(LB[:, 1, :], LB[:, 2, :], LB[:, 3, :], ALU.add))
        link(V.reciprocal(LB[:, 3, :], LB[:, 1, :]))
        link(V.tensor_tensor(LB[:, 4, :], LB[:, 2, :], LB[:, 3, :], ALU.mult))
        link(V.tensor_scalar(LB[:, 5, :], LB[:, 4, :], -1.0, 1.0, ALU.mult, ALU.add))
        dve.wait_ge(sem("mod_fold"), 18)
        for cond in range(2):
            link(V.tensor_tensor(MV[:, :, cond], PP[2][:, 0, 0:2 * NMOD * KT].rearrange("p (a b) -> p a b", b=2)
                                 [:, :, cond], VA[:, 0:NMOD * KT], ALU.add))
        for b in range(3):
            half = 1.0 if b == 1 else 0.5
            for cond in range(2):
                sc = MV[:, (3 * b + 1) * KT:(3 * b + 2) * KT, cond]
                gt = MV[:, (3 * b + 2) * KT:(3 * b + 3) * KT, cond]
                pre = VA[:, 72 + b * KT:72 + (b + 1) * KT]
                post = VA[:, 96 + b * KT:96 + (b + 1) * KT]
                link(V.scalar_tensor_tensor(Avec[:, b, :, cond], sc, 1.0, pre, ALU.add, ALU.mult))
                link(V.scalar_tensor_tensor(Gvec[:, b, :, cond], gt, half, post, ALU.mult, ALU.mult))

        for s in range(2):
            dve.wait_ge(hi_done, s + 1)
            V.tensor_tensor(Wlo[s][:, :, :], raw[s][:, :, :], Whi[s][:, :, :].bitcast(fp32), ALU.subtract)\
                .then_inc(lo_done, 1)

        def make_h(b):
            dve.wait_ge(sem("x_std"), b + 1)
            link(V.reciprocal(RS[:, :], RS[:, :]))

            def scaled(n):
                if n >= 2:
                    dve.wait_ge(sem("h_full"), b * KT + n - 1)
                V.tensor_tensor(BT[n % 2][:, :], XT[:, n, :], RS[:, :], ALU.mult).then_inc(sem("h_scaled"), 1)

            scaled(0)
            for n in range(KT):
                if n + 1 < KT:
                    scaled(n + 1)
                dve.wait_ge(sem("h_hi"), b * KT + n + 1)
                V.tensor_tensor(Hlo[:, n, :], BH[n % 2][:, :], Hhi[:, n, :].bitcast(fp32), ALU.subtract)\
                    .then_inc(sem("h_ready"), 1)

        def boundary(b):
            dve.wait_ge(sem("y_std"), b + 1)
            link(V.reciprocal(RS[:, :], RS[:, :]))
            for n in range(KT):
                link(V.tensor_tensor(BT[n % 2][:, :], Y[:, n, :], RS[:, :], ALU.mult))
                for cond, t0, t1 in TOK:
                    m = V.scalar_tensor_tensor(XT[:, n, t0:t1], BT[n % 2][:, t0:t1], Gvec[:, b, n, cond:cond + 1],
                                               XT[:, n, t0:t1], ALU.mult, ALU.add)
                m.then_inc(sem("x_new"), 1)

        def ffn_in(f):
            ph = PLAN[f"ffn{f}_in"]
            with dve.Fori(0, FT) as j:
                split_lo(ph, j, 0)
                dve.wait_ge(slab_done, ph.slab(j, 1) + 1)
                dve.wait_ge(sem("gate_ready"), j + (f * FT + 2))
                dve.wait_ge(sem("mid_hi"), j + (f * FT + 1))
                dve.wait_ge(sem("mid_lo"), j + (f * FT + 1))
                V.tensor_tensor(two(TT[1][:, :]), two(TT[0][:, :]), halves(1), ALU.mult)\
                    .then_inc(sem("hid_ready"), 1)
                split_lo(ph, j, 1)
                dve.wait_ge(sem("mid_hi"), j + (f * FT + 2))
                V.tensor_tensor(Mlo[:, bass.ds(j, 1), :], TT[1][:, :].rearrange("p (a b) -> p a b", a=1),
                                Mhi[:, bass.ds(j, 1), :].bitcast(fp32), ALU.subtract).then_inc(sem("mid_lo"), 1)

        def acc(j, n2, y0):
            dve.wait_ge(sem("y_sq"), j * 2 + (y0 + n2 + 3))
            dve.wait_ge(sem("acc_done"), j * 2 + (y0 + n2 + 2))
            V.tensor_tensor(TT[2][:, :], TT[2][:, :], TT[n2][:, :], ALU.add).then_inc(sem("acc_done"), 1)

        def ffn_out(f, y0, last=False):
            ph = PLAN[f"ffn{f}_out"]
            link(V.memset(TT[2][:, :], 0.0))
            bodies = ph.bodies - 1 if last else ph.bodies
            with dve.Fori(0, bodies) as j:
                for n2 in range(2):
                    for s in range(3):
                        split_lo(ph, j, 3 * n2 + s)
                    acc(j, n2, y0)
            if last:
                for n2 in range(2):
                    for s in range(3):
                        if 3 * n2 + s < 4:
                            split_lo(ph, bodies, 3 * n2 + s)
                    acc(bodies, n2, y0)

        make_h(0)
        ffn_in(0)
        ffn_out(0, 0)
        boundary(0)
        make_h(1)

        def fourier_im(g):
            dve.wait_ge(sem("v_ready"), g + 1)
            V.tensor_copy(VRI[:, 1, g, P:T], PP[1][:, g % 2, :]).then_inc(sem("v_im"), 1)

        def fourier_lo(g):
            dve.wait_ge(sem("yhi_done"), g + 1)
            V.tensor_tensor(two(Ylo[:, g, :]), halves(3), two(Yhi[:, g, :]).bitcast(fp32), ALU.subtract)\
                .then_inc(sem("ylo_done"), 1)

        ph = PLAN["mix_in"]
        for i in range(24):
            s, section, hd = i % 2, i // NH, i % NH
            split_lo(ph, i // 2, s)
            if section in (0, 4):
                dve.wait_ge(sem("tok_T"), (0 if section == 0 else 4) + hd + 1)
                dst = UT if section == 0 else VT
                V.tensor_copy(dst[:, :, hd * P:(hd + 1) * P],
                              flat(2 + s)[:, 0:T].rearrange("p (a b) -> p a b", a=NCH)).then_inc(sem("t_free"), 1)
            elif section in (1, 5):
                dve.wait_ge(sem("t_ready"), i + 1)
                dst = QD[:, 0, hd, :] if section == 1 else GT[:, hd, :]
                m = V.tensor_tensor(two(dst), two(TT[s][:, :]), halves(s), ALU.mult)
                if section == 1:
                    link(m)
                    m = V.tensor_copy(QD[:, 1, hd, :], QD[:, 0, hd, :])
                m.then_inc(sem("t_free"), 1)
            else:
                dve.wait_ge(sem("t_ready"), i + 1)
                d = section - 2
                col = d * NH + hd
                link(V.tensor_scalar(FD[:, 1 - d, hd, :], TT[s][:, :], LB[:, 5, col:col + 1], LB[:, 4, col:col + 1],
                                     ALU.mult, ALU.add))
                V.tensor_scalar(KD[:, d, hd, :], FD[:, 1 - d, hd, :], -1.0, 1.0, ALU.mult, ALU.add)\
                    .then_inc(sem("t_free"), 1)
            if i == 3:
                for g in range(NH):
                    fourier_im(g)
                    if g >= 1:
                        fourier_lo(g - 1)
                fourier_lo(NH - 1)

        dve.wait_ge(sem("mask_in"), 16)
        V.tensor_copy(mask[:, :, :], maskf[:, :, :]).then_inc(sem("mask_set"), 1)
        dve.wait_ge(sem("mask_set"), 1)

        def blocks(tensor, hd, array, h, side):
            return tensor[:, array, hd, :].rearrange("p (b c) -> p b c", c=2 * h)[:, :, side * h:(side + 1) * h]

        def totals(hd, array, h, side):
            ap = blocks(FD, hd, array, h, side)[:, :, 0:1]
            return ap.to_broadcast([P, T // (2 * h), h]) if h > 1 else ap

        for hp in range(NH // 2):
            for lev in range(8):
                for a in range(2):
                    hd = 2 * hp + a
                    dve.wait_ge(sem("lev_mm"), 16 * hp + 2 * lev + a + 1)
                    if lev == 0:
                        V.tensor_tensor(QD[:, :, hd, :], QD[:, :, hd, :], FD[:, :, hd, :], ALU.mult)\
                            .then_inc(sem("upd_done"), 1)
                        continue
                    h = 1 << (lev - 1)
                    if lev == 1:
                        dve.wait_ge(sem("at_start"), 2 * hp + a + 1)
                    dve.wait_ge(sem("upd_done"), 16 * hp + 2 * (lev - 1) + a + 1)
                    V.tensor_tensor(blocks(QD, hd, 0, h, 0), blocks(QD, hd, 0, h, 0), totals(hd, 0, h, 1), ALU.mult)
                    V.tensor_tensor(blocks(QD, hd, 1, h, 1), blocks(QD, hd, 1, h, 1), totals(hd, 1, h, 0), ALU.mult)
                    V.tensor_tensor(blocks(KD, hd, 0, h, 0), blocks(KD, hd, 0, h, 0), totals(hd, 1, h, 1), ALU.mult)
                    link(V.tensor_tensor(blocks(KD, hd, 1, h, 1), blocks(KD, hd, 1, h, 1), totals(hd, 0, h, 0),
                                         ALU.mult))
                    tot = FD[:, :, hd, :].rearrange("p d (b c) -> p d b c", c=2 * h)
                    V.tensor_tensor(tot[:, :, :, 0], tot[:, :, :, 0], tot[:, :, :, h], ALU.mult)\
                        .then_inc(sem("upd_done"), 1)
                    if lev > 1:
                        dve.wait_ge(sem("at_done"), 14 * hp + 2 * (lev - 2) + a + 1)
                    V.copy_predicated(TT[a][:, :].rearrange("p (a b) -> p a b", a=NCH),
                                      mask[:, lev - 1:lev, :].to_broadcast([P, NCH, P]),
                                      flat(a)[:, 0:T].rearrange("p (a b) -> p a b", a=NCH))\
                        .then_inc(sem("at_done"), 1)
            for a in range(2):
                hd = 2 * hp + a
                dve.wait_ge(sem("state_in"), 32 * (hd + 1))
                dve.wait_ge(sem("so_ready"), hd + 1)
                for e in range(3):
                    m = V.scalar_tensor_tensor(SV[:, 0, e + 1, :], SV[:, 0, e, :],
                                               FD[:, 1, hd, (e + 1) * P:(e + 1) * P + 1],
                                               flat(3)[:, (e + 1) * P:(e + 2) * P], ALU.mult, ALU.add)
                    link(m)
                    m = V.scalar_tensor_tensor(SV[:, 1, e + 1, :], SV[:, 1, e, :],
                                               FD[:, 0, hd, (4 - e) * P:(4 - e) * P + 1],
                                               flat(3)[:, (7 - e) * P:(8 - e) * P], ALU.mult, ALU.add)
                    if e < 2:
                        link(m)
                    else:
                        m.then_inc(sem("sv_done"), 1)
                dve.wait_ge(sem("o_std"), hd + 1)
                link(V.reciprocal(TT[2][:, :], TT[2][:, :]))
                link(V.tensor_tensor(TT[2][:, :], TT[2][:, :], flat(a)[:, 0:T], ALU.mult))
                V.scalar_tensor_tensor(TT[2][:, :], TT[2][:, :], VB[:, hd:hd + 1], GT[:, hd, :], ALU.mult, ALU.mult)\
                    .then_inc(sem("o_full"), 1)
                dve.wait_ge(sem("o_hi"), hd + 1)
                V.tensor_tensor(Olo[:, hd, :], TT[2][:, :], Ohi[:, hd, :].bitcast(fp32), ALU.subtract)\
                    .then_inc(sem("o_done"), 1)

        ph = PLAN["mix_merge"]
        with dve.Fori(0, ph.bodies) as j:
            for n2 in range(2):
                split_lo(ph, j, 3 * n2)
                split_lo(ph, j, 3 * n2 + 1)
                split_lo(ph, j, 3 * n2 + 2)
                dve.wait_ge(slab_done, ph.slab(j, 3 * n2 + 2) + 1)
                dve.wait_ge(sem("gb_ready"), j * 2 + (n2 + 2))
                V.tensor_tensor(two(TT[0][:, :]), two(TT[0][:, :]), halves(2), ALU.mult).then_inc(sem("branch_a"), 1)
                V.tensor_tensor(two(TT[1][:, :]), two(TT[1][:, :]), halves(3), ALU.mult).then_inc(sem("branch_b"), 1)
                dve.wait_ge(sem("branch_a"), j * 2 + (n2 + 1))
                dve.wait_ge(sem("branch_b"), j * 2 + (n2 + 2))
                dve.wait_ge(sem("mg_done"), j * 2 + (n2 + 1))
                V.tensor_tensor(TT[2][:, :], TT[0][:, :], TT[1][:, :], ALU.add).then_inc(sem("mg_ready"), 1)
                dve.wait_ge(sem("mg_hi"), j * 2 + (n2 + 1))
                V.tensor_tensor(MGlo[:, bass.ds(j * 2 + n2, 1), :], TT[2][:, :].rearrange("p (a b) -> p a b", a=1),
                                MGhi[:, bass.ds(j * 2 + n2, 1), :].bitcast(fp32), ALU.subtract)\
                    .then_inc(sem("mg_done"), 1)
        ph = PLAN["mix_out"]
        dve.wait_ge(sem("mg_done"), KT + 1)
        link(V.memset(TT[2][:, :], 0.0))
        with dve.Fori(0, ph.bodies) as j:
            for s in range(2):
                split_lo(ph, j, s)
                acc(j, s, KT)
        dve.wait_ge(sem("state_out"), 32 * NH)
        boundary(1)
        make_h(2)
        ffn_in(1)
        ffn_out(1, 2 * KT, last=True)
        boundary(2)

    block_cm.__exit__(None, None, None)


_INS = ["x_prompt", "x_sample", "state_hgrn", "c", "c_ctx", "w_mod", "b_mod", "norm_pre", "norm_post", "ffn_w_in",
        "ffn_w_out", "w_in", "w_four", "hgrn_gain", "w_hgrn", "w_out", "lb_logits"]
_OUTS = [(1, 128, 1024), (1, 512, 1024), (1, 1, 2, 4, 128, 128)]


def _tables():
    import numpy as np

    n = np.arange(P)
    const = np.zeros((P, P + 2), np.float32)
    const[n, n] = 1.0
    for q in range(4):
        for r in range(2):
            const[32 * q + r, P + r] = 1.0
    turn = 2 * np.pi * (np.outer(n, n) % P) / P
    t = np.arange(LAT)
    row, col = t // 64, t % 64
    turn_lat = 2 * np.pi * ((8 * (row[:, None] * row[None, :] % 8) + col[:, None] * col[None, :] % 64) % 64) / 64
    lat = [f(turn_lat).reshape(4, P, LAT).transpose(1, 0, 2).reshape(P, 4 * LAT) / 256 for f in (np.cos, np.sin)]
    dft = np.concatenate([np.cos(turn), -np.sin(turn), np.cos(turn) / P, np.sin(turn) / P] + lat, axis=1)
    x = n[:, None] ^ n[None, :]
    mask = np.stack([(x >> k) == 1 for k in range(7)], axis=1)
    return {"t_const": const, "t_dft": dft.astype(np.float32), "t_mask": mask.astype(np.float32)}


def kernel(**inputs):
    import numpy as _np
    import concourse.bacc as _bacc
    from concourse import mybir as _mybir
    from concourse.bass_utils import run_bass_kernel_spmd as _run

    nc = _bacc.Bacc("TRN2", target_bir_lowering=False, num_devices=1)
    arrays, args = {}, []
    feed = [(name, _np.ascontiguousarray(inputs[name])) for name in _INS] + list(_tables().items())
    for name, a in feed:
        arrays[f"in_{name}"] = a
        args.append(nc.dram_tensor(f"in_{name}", a.shape, _mybir.dt.from_np(a.dtype), kind="ExternalInput").ap())
    for i, shape in enumerate(_OUTS):
        args.append(nc.dram_tensor(f"out_{i}", shape, _mybir.dt.float32, kind="ExternalOutput").ap())
    hybrid_step_kernel(nc, *args)
    r = _run(nc, [arrays], core_ids=[0])
    return tuple(r.results[0][f"out_{i}"] for i in range(len(_OUTS)))
```

```python
import concourse.bass as bass
from concourse import mybir

P = 128
D = 1024
KT = D // P
CTX, LAT = 128, 512
T = CTX + LAT
HALF = T // 2
NCH = T // P
DFF = 2816
FT = DFF // P
NH = 4
NMOD = 9
EPS = 1e-6
TB = T * 4
W_IN_GATES = 3072

fp32 = mybir.dt.float32
fp32r = mybir.dt.float32r
u8 = mybir.dt.uint8
ACT = mybir.ActivationFunctionType
ALU = mybir.AluOpType

PHASES = [
    ("ffn0_in", FT, [1, 1]),
    ("ffn0_out", KT // 2, [1] * 6),
    ("mix_heads", NH // 2, [1] * 10),
    ("mix_u", NH // 2, [1, 1]),
    ("mix_merge", KT // 2, [1, 1, 2, 1, 1, 2]),
    ("mix_out", KT // 2, [1, 1]),
    ("ffn1_in", FT, [1, 1]),
    ("ffn1_out", KT // 2, [1] * 6),
]
MOD_EARLY = 4
MOD_LATE = NMOD * D // 512 - MOD_EARLY
MOD_LATE_FREE = MOD_LATE
HEAD_COLS = [512, 1024, 1536, 2048, 2560]
KEYS = [(0, 0), (0, 1), (0, 2), (0, 3), (1, 0), (1, 2), (1, 3), (1, 4)]
OUT_SPLIT = [(0, 8), (8, 7), (15, 7)]


class Phase:

    def __init__(self, slabs, dmas, bodies, kinds):
        self.base, self.raw0, self.bodies, self.kinds = slabs, list(dmas), bodies, kinds
        self.per = len(kinds)
        self.raw_per = [16 * sum(k for n, k in enumerate(kinds) if n % 2 == s) for s in (0, 1)]

    def slab(self, body, pos):
        return body * self.per + (self.base + pos)

    def raw_need(self, body, pos):
        body, pos = body + pos // self.per, pos % self.per
        s = pos % 2
        within = 16 * sum(k for n, k in enumerate(self.kinds[:pos + 1]) if n % 2 == s)
        return body * self.raw_per[s] + (self.raw0[s] + within)


def plan():
    out, slabs, dmas = {}, 0, [0, 0]
    for name, bodies, kinds in PHASES:
        ph = Phase(slabs, dmas, bodies, kinds)
        out[name] = ph
        slabs += bodies * ph.per
        dmas = [dmas[s] + bodies * ph.raw_per[s] for s in (0, 1)]
    return out, slabs


def hybrid_step_kernel(nc, x_prompt, x_sample, state_hgrn, c, c_ctx, w_mod, b_mod, norm_pre, norm_post,
                       ffn_w_in, ffn_w_out, w_in, w_four, hgrn_gain, w_hgrn, w_out, lb_logits,
                       t_const, t_dft, t_mask, y_prompt, y_sample, new_state):
    PLAN, NSLAB = plan()

    top = [(nc.sbuf_base + 31) // 32 * 32]

    def place(name, shape, dtype, at=None):
        size = mybir.dt.size(dtype)
        for n in shape[1:]:
            size *= n
        if at is None:
            at = top[0]
            top[0] = (at + size + 31) // 32 * 32
        return nc.alloc_sbuf_tensor_at(name, shape, dtype, offset=at)

    XT = place("XT", [P, KT, T], fp32)
    h_at = top[0]
    Hhi = place("Hhi", [P, KT, T], fp32r)
    Hlo = place("Hlo", [P, KT, T], fp32r)
    Y = place("Y", [P, KT, T], fp32, at=h_at)
    mid_at = top[0]
    Mhi = place("Mhi", [P, FT, T], fp32r)
    Mlo = place("Mlo", [P, FT, T], fp32r)
    raw = [place(f"raw{s}", [P, KT, P], fp32) for s in (0, 1)]
    Whi = [place(f"Whi{s}", [P, KT, P], fp32r) for s in (0, 1)]
    Wlo = [place(f"Wlo{s}", [P, KT, P], fp32r) for s in (0, 1)]
    TT = [place(f"TT{s}", [P, T], fp32) for s in (0, 1, 2)]
    ident = place("ident", [P, P + 2], fp32)
    ones_d = place("ones_d", [P, P], fp32)
    ones_h = place("ones_h", [P, P], fp32)
    VA = place("VA", [P, 120], fp32)
    VB = place("VB", [P, 36], fp32)
    MV = place("MV", [P, NMOD * KT, 2], fp32)
    Avec = place("Avec", [P, 3, KT, 2], fp32)
    Gvec = place("Gvec", [P, 3, KT, 2], fp32)
    LB = place("LB", [P, 6, 8], fp32)
    mask = place("mask", [P, 7, P], u8)
    S2 = place("S2", [P, KT, 32], fp32)
    assert top[0] <= nc.sbuf_usable_end, (top[0], nc.sbuf_usable_end)

    def tile_at(n):
        return mid_at + n * TB

    xtok = place("xtok", [P, NCH, D], fp32, at=tile_at(0))
    rowsA = place("rowsA", [120, P], fp32, at=tile_at(8))
    rowsB = place("rowsB", [36, P], fp32, at=tile_at(8) + 512)
    modrow = [place(f"modrow{s}", [P, 512], fp32, at=tile_at(9) + 2048 * s) for s in (0, 1)]
    modw = [place(f"modw{s}", [P, KT, 512], fp32, at=tile_at(11) + 16384 * s) for s in range(4)]
    late_at = [tile_at(MOD_LATE_FREE), tile_at(FT + MOD_LATE_FREE)]
    modl = [place(f"modl{s}", [P, KT, 512], fp32, at=late_at[s]) for s in (0, 1)]
    modrowl = [place(f"modrowl{s}", [P, 512], fp32, at=late_at[s] + 16384) for s in (0, 1)]
    BT = [place(f"BT{s}", [P, T], fp32, at=tile_at(n)) for s, n in enumerate((37, 38, 39, 40, 42, 43))]
    BH = BT[3:6]
    RS = place("RS", [P, T], fp32, at=tile_at(41))
    OUTB = place("OUTB", [P, NCH, D], fp32, at=tile_at(0))
    Yhi = place("Yhi", [P, NH, T], fp32r, at=tile_at(0))
    Ylo = place("Ylo", [P, NH, T], fp32r, at=tile_at(4))
    UT = [place(f"UT{g}", [P, NCH, P], fp32, at=tile_at(18 + 4 * g)) for g in range(NH)]
    VRI = [place(f"VRI{g}", [P, 2, T], fp32, at=tile_at(n)) for g, n in enumerate((32, 34, 37, 40))]
    DFTS = place("DFTS", [P, 512], fp32, at=tile_at(36))
    DFTL = [[place(f"DFTL{part}{a}", [P, 512], fp32, at=tile_at(16 + 8 * part + 4 * (a // 2) + a % 2))
             for a in range(4)] for part in range(2)]
    QD = place("QD", [P, 2, NH, T], fp32, at=tile_at(8))
    KD = place("KD", [P, 2, NH, T], fp32, at=tile_at(16))
    FD = place("FD", [P, 2, NH, T], fp32, at=tile_at(24))
    VT = place("VT", [P, NCH, 512], fp32, at=tile_at(32))
    GT = place("GT", [P, NH, T], fp32, at=tile_at(36))
    AT = place("AT", [P, T], fp32, at=tile_at(0))
    KX = [place(f"KX{n}", [P, T], fp32, at=tile_at(1 + n)) for n in range(2)]
    OT = place("OT", [P, T], fp32, at=tile_at(3))
    maskf = place("maskf", [P, 7, P], fp32, at=tile_at(4))
    KTOK = place("KTOK", [P, 8, P], fp32, at=tile_at(40))
    SV = place("SV", [P, 2, 4, P], fp32, at=tile_at(40) + 4096)
    SO = place("SO", [P, 2, P], fp32, at=tile_at(40) + 8192)
    Ohi = place("Ohi", [P, NH, T], fp32r, at=tile_at(8))
    Olo = place("Olo", [P, NH, T], fp32r, at=tile_at(12))
    MGhi = place("MGhi", [P, KT, T], fp32r, at=tile_at(16))
    MGlo = place("MGlo", [P, KT, T], fp32r, at=tile_at(24))

    PP = [nc.alloc_psum_tensor(f"PP{n}", [P, 2, 512], fp32) for n in range(4)]

    def halves(n):
        return PP[n][:, :, 0:HALF]

    def flat(n):
        return PP[n][:, :, :].rearrange("p a b -> p (a b)")

    def two(ap):
        return ap.rearrange("p (a b) -> p a b", a=2)

    sems = {}

    def sem(name):
        if name not in sems:
            sems[name] = nc.alloc_semaphore(name)
        return sems[name]

    raw_full = [sem("raw_full0"), sem("raw_full1")]
    hi_done, lo_done = sem("hi_done"), sem("lo_done")
    slab_done = sem("slab_done")

    TOK = [(0, 0, CTX), (1, CTX, T)]

    def level_ap(tensor, hd, first, tokens, h):
        base = tensor[:, 0, hd, first:first + tokens]
        return bass.AP(base.tensor, base.offset,
                       [[2 * NH * T, P], [2 * h, tokens // (2 * h)], [NH * T + h, 2], [1, h]])

    def pair_of(hd, lev):
        return 2 + (hd + lev) % 2

    block_cm = nc.Block()
    block = block_cm.__enter__()

    @block.sync
    def _(sp):
        sp.dma_start(ident[:, :], t_const).then_inc(sem("const_in"), 16)
        sp.dma_start(rowsA[0:72, :], b_mod.rearrange("l (r q) -> (l r) q", q=P)).then_inc(sem("rows_in"), 16)
        sp.dma_start(rowsA[72:96, :], norm_pre.rearrange("l s (r q) -> (l s r) q", q=P)).then_inc(sem("rows_in"), 16)
        sp.dma_start(rowsA[96:120, :], norm_post.rearrange("l s (r q) -> (l s r) q", q=P)).then_inc(sem("rows_in"), 16)
        sp.dma_start(rowsB[0:4, :], hgrn_gain.rearrange("l (r q) -> (l r) q", q=P)).then_inc(sem("rows_in"), 16)
        sp.dma_start(rowsB[4:20, :], lb_logits.rearrange("l d (r q) -> (l d r) q", q=P)).then_inc(sem("rows_in"), 16)
        sp.dma_start(rowsB[20:28, :], c.rearrange("l (r q) -> (l r) q", q=P)).then_inc(sem("rows_in"), 16)
        sp.dma_start(rowsB[28:36, :], c_ctx.rearrange("(r q) -> r q", q=P)).then_inc(sem("rows_in"), 16)
        sp.dma_start(xtok[:, 0, :], x_prompt[0]).then_inc(sem("x_in"), 16)
        sp.dma_start(xtok[:, 1:NCH, :], x_sample[0].rearrange("(a p) f -> p a f", p=P)).then_inc(sem("x_in"), 16)
        wm = w_mod[0].rearrange("(k p) n -> p k n", p=P)
        for i in range(4):
            sp.dma_start(modw[i][:, :, :], wm[:, :, i * 512:(i + 1) * 512]).then_inc(sem(f"modw_in{i}"), 16)
        def load(ph, body, pos, parts, first=False):
            if not first:
                sp.wait_ge(lo_done, ph.slab(body, pos) - 1)
            for k0, kn, src in parts:
                sp.dma_start(raw[pos % 2][:, k0:k0 + kn, :], src).then_inc(raw_full[pos % 2], 16)

        def col(ap, start):
            return ap[:, :, bass.ds(start, P)]

        def ffn_in_pair(ph, w, j, first=False):
            load(ph, j, 0, [(0, KT, col(w, j * P))], first)
            load(ph, j, 1, [(0, KT, col(w, j * P + DFF))], first)

        def load_mod(i, s):
            sp.dma_start(modl[s][:, :, :], wm[:, :, bass.ds(i * 512, 512)]).then_inc(sem(f"modl_in{s}"), 16)

        def load_ffn_in(f):
            ph = PLAN[f"ffn{f}_in"]
            w = ffn_w_in[0, f].rearrange("(k p) n -> p k n", p=P)
            if f == 0:
                ffn_in_pair(ph, w, 0, first=True)
                sp.wait_ge(sem("mod_mm"), MOD_EARLY)
                sp.wait_ge(sem("h_ready"), KT)
                load_mod(MOD_EARLY, 0)
                load_mod(MOD_EARLY + 1, 1)
                with sp.Fori(0, MOD_LATE // 2 - 1) as jj:
                    for s in range(2):
                        ffn_in_pair(ph, w, jj * 2 + (1 + s))
                        sp.wait_ge(sem("mod_mm"), jj * 2 + (MOD_EARLY + s + 1))
                        load_mod(jj * 2 + (MOD_EARLY + 2 + s), s)
                with sp.Fori(MOD_LATE - 1, FT) as j:
                    ffn_in_pair(ph, w, j)
            else:
                with sp.Fori(0, FT) as j:
                    ffn_in_pair(ph, w, j)

        def load_ffn_out(f):
            ph = PLAN[f"ffn{f}_out"]
            w = ffn_w_out[0, f].rearrange("(k p) n -> p k n", p=P)
            with sp.Fori(0, ph.bodies) as j:
                for n2 in range(2):
                    for s, (k0, kn) in enumerate(OUT_SPLIT):
                        load(ph, j, 3 * n2 + s, [(0, kn, w[:, k0:k0 + kn, bass.ds(j * 2 * P + n2 * P, P)])])

        load_ffn_in(0)
        load_ffn_out(0)
        wi = w_in[0].rearrange("(k p) n -> p k n", p=P)
        ph = PLAN["mix_heads"]
        with sp.Fori(0, ph.bodies) as hp:
            for a in range(2):
                for n, first_col in enumerate(HEAD_COLS):
                    load(ph, hp, 5 * a + n, [(0, KT, col(wi, hp * 2 * P + (first_col + a * P)))])
        ph = PLAN["mix_u"]
        with sp.Fori(0, ph.bodies) as j:
            for s in range(2):
                load(ph, j, s, [(0, KT, col(wi, j * 2 * P + s * P))])
        ph = PLAN["mix_merge"]
        w4 = w_four[0].rearrange("(k p) n -> p k n", p=P)
        wh = w_hgrn[0].rearrange("(k p) n -> p k n", p=P)
        with sp.Fori(0, ph.bodies) as j:
            for n2 in range(2):
                at = j * 2 * P + n2 * P
                load(ph, j, 3 * n2, [(0, KT, col(wi, at + W_IN_GATES))])
                load(ph, j, 3 * n2 + 1, [(0, KT, col(wi, at + (W_IN_GATES + D)))])
                load(ph, j, 3 * n2 + 2, [(0, NH, col(w4, (j * P + n2 * (P // 2)) * 2)), (NH, NH, col(wh, at))])
        ph = PLAN["mix_out"]
        wo = w_out[0].rearrange("(k p) n -> p k n", p=P)
        with sp.Fori(0, ph.bodies) as j:
            for s in range(2):
                load(ph, j, s, [(0, KT, col(wo, j * 2 * P + s * P))])
        load_ffn_in(1)
        load_ffn_out(1)
        for part in range(2):
            sp.wait_ge(sem("out_tile"), 4 * (part + 1))
            cols = slice(512 * part, 512 * (part + 1))
            sp.dma_start(y_prompt[0][:, cols], OUTB[:, 0, cols]).then_inc(sem("y_out"), 16)
            sp.dma_start(y_sample[0].rearrange("(a p) f -> p a f", p=P)[:, :, cols],
                         OUTB[:, 1:NCH, cols]).then_inc(sem("y_out"), 16)
        sp.wait_ge(sem("y_out"), 64)


    @block.gpsimd
    def _(pool):
        def split_lo(first, count):
            with pool.Fori(0, count // 2) as j:
                for s in range(2):
                    pool.wait_ge(hi_done, j * 2 + (first + s + 1))
                    nc.gpsimd.tensor_tensor(Wlo[s][:, :, :], raw[s][:, :, :], Whi[s][:, :, :].bitcast(fp32),
                                            ALU.subtract).then_inc(lo_done, 1)

        def boundary(b):
            for n in range(1, KT, 2):
                pool.wait_ge(sem("y_scaled"), b * KT + n + 1)
                nc.gpsimd.tensor_tensor(XT[:, n, :], XT[:, n, :], BT[n % 6][:, :], ALU.add)\
                    .then_inc(sem("x_new1"), 1)

        first = 0
        for b, name in enumerate(("mix_heads", "ffn1_in", None)):
            until = PLAN[name].base + 2 if name else NSLAB
            split_lo(first, until - first)
            boundary(b)
            first = until
    @block.tensor
    def _(pe):
        mm = nc.tensor.matmul

        def slab(ph, body, pos, rhs, outs, k_total=KT, first_slab=True, last_slab=True):
            pe.wait_ge(lo_done, ph.slab(body, pos) + 1)
            s = pos % 2
            count = {}
            last = None
            for k, ((hi, lo), out) in enumerate(zip(rhs, outs)):
                n = outs.count(out)
                seen = count.get(out, 0)
                count[out] = seen + 1
                for a, (w, x) in enumerate(((Whi[s], hi), (Whi[s], lo), (Wlo[s], hi))):
                    for half in range(2):
                        last = mm(PP[out][:, half, 0:HALF], w[:, k, :], x[:, half * HALF:(half + 1) * HALF],
                                  start=first_slab and seen == 0 and a == 0,
                                  stop=last_slab and seen == n - 1 and a == 2)
            last.then_inc(slab_done, 1)

        def first_slabs(ph, b):
            for s in range(2):
                pe.wait_ge(lo_done, ph.slab(0, s) + 1)
            for k in range(KT):
                pe.wait_ge(sem("h_ready"), b * KT + k + 1)
                hi, lo = h_tiles[k]
                for s in range(2):
                    for a, (w, x) in enumerate(((Whi[s], hi), (Whi[s], lo), (Wlo[s], hi))):
                        for half in range(2):
                            m = mm(PP[s][:, half, 0:HALF], w[:, k, :], x[:, half * HALF:(half + 1) * HALF],
                                   start=k == 0 and a == 0, stop=k == KT - 1 and a == 2)
                    if k == KT - 1:
                        m.then_inc(slab_done, 1)

        h_tiles = [(Hhi[:, k, :], Hlo[:, k, :]) for k in range(KT)]

        def stat(src, n, out, one, first=True, last=True):
            for half in range(2):
                m = mm(PP[out][:, half, 0:HALF], one[:, :], src[:, half * HALF:(half + 1) * HALF],
                       start=first, stop=last)
            return m

        def transpose(out, in_):
            k = in_.shape[0]
            return nc.tensor.transpose(out, in_, ident[0:k, 0:k])

        pe.wait_ge(sem("const_in"), 16)
        pe.wait_ge(sem("rows_in"), 16 * 7)
        transpose(PP[2][:, 0, 0:120], rowsA[:, :]).then_inc(sem("vec_T"), 1)
        transpose(PP[2][:, 1, 0:36], rowsB[:, :]).then_inc(sem("vec_T"), 1)
        pe.wait_ge(sem("x_in"), 32)
        pe.wait_ge(sem("ones_set"), 2)
        for n in range(KT):
            if n >= 2:
                pe.wait_ge(sem("x_sq"), n - 1)
            for ch in range(NCH):
                m = transpose(flat(n % 2)[:, ch * P:(ch + 1) * P], xtok[:, ch, n * P:(n + 1) * P])
            m.then_inc(sem("x_T"), 1)
            if n >= 1:
                pe.wait_ge(sem("x_sq"), n)
                stat(TT[(n - 1) % 2], n - 1, 3, ones_d, n == 1, False).then_inc(sem("x_stat"), 1)
        pe.wait_ge(sem("x_sq"), KT)
        stat(TT[(KT - 1) % 2], KT - 1, 3, ones_d, False, True).then_inc(sem("x_stat"), 1)
        pe.wait_ge(sem("silu_c"), 2)

        def mod_slab(i, w, bank):
            for k in range(KT):
                q = k % 4
                m = mm(PP[3][32 * q:32 * q + 32, bank, :], S2[:, k, :], w[:, k, :], start=k < 4, stop=k >= 4)
            m.then_inc(sem("mod_mm"), 1)

        def fold_mod(i, rows):
            pe.wait_ge(sem("modrow"), i + 1)
            for q in range(4):
                m = mm(PP[2][:, 0, bass.ds(i * 8 + 2 * q, 2)], rows[:, q * P:(q + 1) * P],
                       ident[:, P:P + 2], start=True, stop=True)
            m.then_inc(sem("mod_fold"), 1)

        pe.wait_ge(sem("x_std"), 1)
        for i in range(MOD_EARLY):
            pe.wait_ge(sem(f"modw_in{i}"), 16)
            if i >= 2:
                pe.wait_ge(sem("modrow"), i - 1)
            mod_slab(i, modw[i], i % 2)
            if i >= 1:
                fold_mod(i - 1, modrow[(i - 1) % 2])
        fold_mod(MOD_EARLY - 1, modrow[(MOD_EARLY - 1) % 2])

        def ffn_in(f):
            ph = PLAN[f"ffn{f}_in"]

            def step(j, mod=None):
                if mod is not None:
                    jj, s = mod
                    pe.wait_ge(sem(f"modl_in{s}"), jj * 16 + 16)
                    pe.wait_ge(sem("modrow"), j + (MOD_EARLY - 1))
                    mod_slab(None, modl[s], s)
                pe.wait_ge(sem("gate_ready"), j + (f * FT + 1))
                slab(ph, j, 0, h_tiles, [0] * KT)
                if mod is not None:
                    fold_mod(j + MOD_EARLY, modrowl[s])
                pe.wait_ge(sem("hid_ready"), j + (f * FT + 1))
                slab(ph, j, 1, h_tiles, [1] * KT)

            first_slabs(ph, 2 * f)
            if f == 0:
                pe.wait_ge(sem("modl_in0"), 16)
                mod_slab(None, modl[0], 0)
                fold_mod(MOD_EARLY, modrowl[0])
                step(1, (0, 1))
                with pe.Fori(1, MOD_LATE // 2) as jj:
                    for s in range(2):
                        step(jj * 2 + s, (jj, s))
                with pe.Fori(MOD_LATE, FT) as j:
                    step(j)
            else:
                with pe.Fori(1, FT) as j:
                    step(j)

        def ffn_out(f, y0):
            ph = PLAN[f"ffn{f}_out"]
            with pe.Fori(0, ph.bodies) as j:
                for n2 in range(2):
                    pe.wait_ge(sem("y_sq"), j * 2 + (y0 + n2 + 1))
                    for s, (k0, kn) in enumerate(OUT_SPLIT):
                        pe.wait_ge(sem("mid_lo"), f * FT + k0 + kn + 1)
                        slab(ph, j, 3 * n2 + s, [(Mhi[:, k, :], Mlo[:, k, :]) for k in range(k0, k0 + kn)],
                             [n2] * kn, first_slab=s == 0, last_slab=s == 2)

        def boundary(b, y0, last=False):
            pe.wait_ge(sem("acc_done"), y0 + KT + 2)
            stat(TT[2], 0, 2, ones_d).then_inc(sem("y_stat"), 1)
            if last:
                for n in range(KT):
                    pe.wait_ge(sem(f"x_new{n % 2}"), (b * KT + n) // 2 + 1)
                    if n >= 2:
                        pe.wait_ge(sem("out_tile"), n - 1)
                    for ch in range(NCH):
                        m = transpose(flat(n % 2)[:, ch * P:(ch + 1) * P], XT[:, n, ch * P:(ch + 1) * P])
                    m.then_inc(sem("out_T"), 1)
                return
            for n in range(KT):
                pe.wait_ge(sem("x_sq"), (b + 1) * KT + n + 1)
                stat(TT[n % 2], n, 3, ones_d, n == 0, n == KT - 1).then_inc(sem("x_stat"), 1)

        ffn_in(0)
        ffn_out(0, 0)
        boundary(0, 0)

        heads, first = PLAN["mix_heads"], PLAN["mix_heads"].base

        def quarter(i, part):
            s = i % 2
            if part == 0:
                pe.wait_ge(lo_done, first + i + 1)
                pe.wait_ge(sem("t_free"), i + 1)
            for k in (2 * part, 2 * part + 1):
                hi, lo = h_tiles[k]
                for a, (w, x) in enumerate(((Whi[s], hi), (Whi[s], lo), (Wlo[s], hi))):
                    for half in range(2):
                        m = mm(PP[s][:, half, 0:HALF], w[:, k, :], x[:, half * HALF:(half + 1) * HALF],
                               start=k == 0 and a == 0, stop=k == KT - 1 and a == 2)
            if part == 3:
                m.then_inc(slab_done, 1)

        def token_major(i):
            s = i % 2
            pe.wait_ge(sem("t_ready"), i + 1)
            for ch in range(NCH):
                m = transpose(flat(s)[:, ch * P:(ch + 1) * P], TT[s][:, ch * P:(ch + 1) * P])
            m.then_inc(sem("tok_T"), 1)

        def diagonal(hd):
            pe.wait_ge(sem("ks_ready"), hd + 1)
            if hd:
                pe.wait_ge(sem("o_std"), hd)
            for ch in range(NCH):
                cols = slice(ch * P, (ch + 1) * P)
                m = mm(flat(pair_of(hd, 0))[:, cols], KX[0][:, cols], QD[:, 0, hd, cols], start=True, stop=True)
            m.then_inc(sem("lev_mm"), 1)

        def level(hd, lev):
            pe.wait_ge(sem("kx_ready"), 7 * hd + lev)
            pe.wait_ge(sem("upd_done"), 8 * hd + lev)
            if lev == 1:
                if hd:
                    pe.wait_ge(sem("o_full"), hd)
            elif lev == 2:
                pe.wait_ge(sem("at_start"), hd + 1)
            else:
                pe.wait_ge(sem("at_done"), 7 * hd + lev - 2)
            for ch in range(NCH):
                m = mm(flat(pair_of(hd, lev))[:, ch * P:(ch + 1) * P], KX[lev % 2][:, ch * P:(ch + 1) * P],
                       level_ap(QD, hd, ch * P, P, 1 << (lev - 1)), start=True, stop=True)
            m.then_inc(sem("lev_mm"), 1)

        def keys_to_tokens(hd):
            pe.wait_ge(sem("upd_done"), 8 * hd + 8)
            pe.wait_ge(sem("at_done"), 7 * hd + 6)
            for e, (d, ch) in enumerate(KEYS):
                m = transpose(flat(pair_of(hd, 0))[:, e * P:(e + 1) * P], KD[:, d, hd, ch * P:(ch + 1) * P])
            m.then_inc(sem("kT"), 1)

        def key_values(hd):
            pe.wait_ge(sem("ktok"), hd + 1)
            pe.wait_ge(sem("t_free"), 5 * hd + 4 + 2)
            pe.wait_ge(sem("at_done"), 7 * hd + 7)
            for e, (d, ch) in enumerate(KEYS):
                m = mm(flat(pair_of(hd, 1))[:, e * P:(e + 1) * P], KTOK[:, e, :], VT[:, ch, hd * P:(hd + 1) * P],
                       start=True, stop=True)
            m.then_inc(sem("kv_mm"), 1)

        def outputs(hd):
            pe.wait_ge(sem("sv_done"), hd + 1)
            for ch in range(NCH):
                out = flat(pair_of(hd, 0))[:, ch * P:(ch + 1) * P]
                m = mm(out, VT[:, ch, hd * P:(hd + 1) * P], AT[:, ch * P:(ch + 1) * P], start=True, stop=ch == 0)
                if ch:
                    mm(out, SV[:, 0, ch - 1, :], QD[:, 1, hd, ch * P:(ch + 1) * P], start=False, stop=False)
                    m = mm(out, SV[:, 1, 4 - ch, :], QD[:, 0, hd, ch * P:(ch + 1) * P], start=False, stop=True)
            m.then_inc(sem("o_mm"), 1)

        def output_stat(hd):
            pe.wait_ge(sem("o_sq"), hd + 1)
            stat(OT, 0, pair_of(hd, 1), ones_h).then_inc(sem("o_stat"), 1)

        first_slabs(heads, 1)
        for h in range(NH + 1):
            for t in range(20 if h < NH else 16):
                if h or t >= 8:
                    quarter(5 * h + t // 4, t % 4)
                if h and t % 2 and t <= 11:
                    level(h - 1, (t + 3) // 2)
                if h and t == 12:
                    keys_to_tokens(h - 1)
                if h and t == 13:
                    key_values(h - 1)
                if h and t == 15:
                    outputs(h - 1)
                if h and t == 16:
                    output_stat(h - 1)
                if h < NH and t == 17:
                    diagonal(h)
                if h < NH and t == 18:
                    token_major(5 * h + 3)
                if h < NH and t == 19:
                    level(h, 1)
                if h == NH and t >= 5 and t % 4 == 1:
                    token_major(5 * NH + (t - 5) // 4)
        output_stat(NH - 1)
        token_major(5 * NH + 3)

        pe.wait_ge(sem("dft_in"), 16 * 9)
        pe.wait_ge(sem("t_free"), 24 + 2)
        pe.wait_ge(sem("o_full"), NH)

        def pos_dft(g):
            if g >= 2:
                pe.wait_ge(sem("v_re"), g - 1)
                pe.wait_ge(sem("v_im"), g - 1)
            pr, bank = 2 * (g % 2), g % 2
            mm(PP[pr][:, 0, 0:P], UT[g][:, 0, :], DFTS[:, 256:384], start=True, stop=True)
            mm(PP[pr][:, 0, P:2 * P], UT[g][:, 0, :], DFTS[:, 384:512], start=True, stop=True)
            for part, out in ((0, PP[pr][:, 1, :]), (1, PP[1][:, bank, :])):
                for a in range(4):
                    m = mm(out, UT[g][:, 1 + a, :], DFTL[part][a][:, :], start=a == 0, stop=a == 3)
            m.then_inc(sem("v_ready"), 1)

        def ch_dft(g):
            pe.wait_ge(sem("v_re"), g + 1)
            pe.wait_ge(sem("v_im"), g + 1)
            if g:
                pe.wait_ge(sem("ylo_done"), g)
            for half in range(2):
                cols = slice(half * HALF, (half + 1) * HALF)
                mm(PP[3][:, half, 0:HALF], DFTS[:, 0:P], VRI[g][:, 0, cols], start=True, stop=False)
                m = mm(PP[3][:, half, 0:HALF], DFTS[:, P:2 * P], VRI[g][:, 1, cols], start=False, stop=True)
            m.then_inc(sem("yf_ready"), 1)

        pos_dft(0)
        pos_dft(1)
        ch_dft(0)
        pos_dft(2)
        ch_dft(1)
        pos_dft(3)
        ch_dft(2)
        ch_dft(3)

        ph = PLAN["mix_merge"]
        fh = [(Yhi[:, k, :], Ylo[:, k, :]) for k in range(NH)] + [(Ohi[:, k, :], Olo[:, k, :]) for k in range(NH)]
        with pe.Fori(0, ph.bodies) as j:
            for n2 in range(2):
                pe.wait_ge(sem("ga_ready"), j * 2 + (n2 + 1))
                slab(ph, j, 3 * n2, h_tiles, [0] * KT)
                pe.wait_ge(sem("gb_ready"), j * 2 + (n2 + 1))
                slab(ph, j, 3 * n2 + 1, h_tiles, [1] * KT)
                pe.wait_ge(sem("ylo_done"), NH)
                pe.wait_ge(sem("o_done"), NH)
                pe.wait_ge(sem("branch_b"), j * 2 + (n2 + 1))
                slab(ph, j, 3 * n2 + 2, fh, [2] * NH + [3] * NH)
        pe.wait_ge(sem("mg_done"), KT + 1)
        ph = PLAN["mix_out"]
        mg = [(MGhi[:, k, :], MGlo[:, k, :]) for k in range(KT)]
        with pe.Fori(0, ph.bodies) as j:
            for s in range(2):
                pe.wait_ge(sem("y_sq"), j * 2 + (KT + s + 1))
                slab(ph, j, s, mg, [s] * KT)
        boundary(1, KT)
        ffn_in(1)
        ffn_out(1, 2 * KT)
        boundary(2, 2 * KT, last=True)

    @block.scalar
    def _(act):
        A = nc.scalar.activation

        def split_hi(ph, body, pos):
            act.wait_ge(raw_full[pos % 2], ph.raw_need(body, pos + 2))
            A(Whi[pos % 2][:, :, :], raw[pos % 2][:, :, :], ACT.Copy).then_inc(hi_done, 1)

        def slab_wait(ph, body, pos):
            act.wait_ge(slab_done, ph.slab(body, pos) + 1)

        act.wait_ge(sem("vec_T"), 2)
        act.wait_ge(sem("s2_zero"), 1)
        A(VA[:, :], PP[2][:, 0, 0:120], ACT.Copy).then_inc(sem("vec_evac"), 1)
        A(VB[:, :], PP[2][:, 1, 0:36], ACT.Copy).then_inc(sem("vec_evac"), 1)
        A(TT[2][:, 1:2], PP[2][:, 0, 0:1], ACT.Copy).then_inc(sem("gate_ready"), 1)
        A(TT[2][:, 2:3], PP[2][:, 0, 0:1], ACT.Copy).then_inc(sem("mid_hi"), 1)
        A(TT[2][:, 3:4], PP[2][:, 0, 0:1], ACT.Copy).then_inc(sem("ga_ready"), 1)
        A(TT[2][:, 4:5], PP[2][:, 0, 0:1], ACT.Copy).then_inc(sem("gb_ready"), 1)
        A(TT[2][:, 5:6], PP[2][:, 0, 0:1], ACT.Copy).then_inc(sem("y_sq"), 2)
        A(S2[:, :, 0], PP[2][:, 1, 28:36], ACT.Silu).then_inc(sem("silu_c"), 1)
        A(S2[:, :, 1], PP[2][:, 1, 20:28], ACT.Silu).then_inc(sem("silu_c"), 1)
        act.wait_ge(sem("lb_max"), 1)
        A(LB[:, 2:4, :], LB[:, 2:4, :], ACT.Exp).then_inc(sem("lb_exp"), 1)
        for n in range(KT):
            act.wait_ge(sem("x_T"), n + 1)
            A(XT[:, n, :], flat(n % 2)[:, 0:T], ACT.Copy)
            if n >= 2:
                act.wait_ge(sem("x_stat"), n - 1)
            A(TT[n % 2][:, :], flat(n % 2)[:, 0:T], ACT.Square).then_inc(sem("x_sq"), 1)
        act.wait_ge(sem("x_stat"), KT)
        A(two(RS[:, :]), halves(3), ACT.Sqrt, bias=EPS).then_inc(sem("x_std"), 1)

        def mod_rows(i, s, rows):
            act.wait_ge(sem("mod_mm"), i + 1)
            A(rows[:, :], PP[3][:, s, :], ACT.Copy).then_inc(sem("modrow"), 1)

        for i in range(MOD_EARLY):
            if i >= 2:
                act.wait_ge(sem("mod_fold"), i - 1)
            mod_rows(i, i % 2, modrow[i % 2])
        ph = PLAN["ffn0_in"]
        for s in range(2):
            act.wait_ge(raw_full[s], 16)
            A(Whi[s][:, :, :], raw[s][:, :, :], ACT.Copy).then_inc(hi_done, 1)

        def make_h(b):
            if b:
                act.wait_ge(sem("x_stat"), (b + 1) * KT)
                A(two(RS[:, :]), halves(3), ACT.Sqrt, bias=EPS).then_inc(sem("x_std"), 1)
            else:
                act.wait_ge(sem("mod_set"), 1)

            def full(n):
                act.wait_ge(sem("h_scaled"), b * KT + n + 1)
                if n >= 3:
                    act.wait_ge(sem("h_ready"), b * KT + n - 2)
                for cond, t0, t1 in TOK:
                    m = A(BH[n % 3][:, t0:t1], BT[n % 3][:, t0:t1], ACT.Identity,
                          bias=MV[:, 3 * b * KT + n, cond:cond + 1], scale=Avec[:, b, n, cond:cond + 1])
                m.then_inc(sem("h_full"), 1)

            full(0)
            for n in range(KT):
                if n + 1 < KT:
                    full(n + 1)
                act.wait_ge(sem("h_full"), b * KT + n + 1)
                A(Hhi[:, n, :], BH[n % 3][:, :], ACT.Copy).then_inc(sem("h_hi"), 1)

        def boundary(b, last=False):
            act.wait_ge(sem("y_stat"), b + 1)
            A(two(RS[:, :]), halves(2), ACT.Sqrt, bias=EPS).then_inc(sem("y_std"), 1)
            for n in range(KT):
                if last:
                    act.wait_ge(sem("out_T"), n + 1)
                    A(OUTB[:, :, n * P:(n + 1) * P], flat(n % 2)[:, 0:T].rearrange("p (a b) -> p a b", a=NCH),
                      ACT.Copy).then_inc(sem("out_tile"), 1)
                else:
                    act.wait_ge(sem(f"x_new{n % 2}"), (b * KT + n) // 2 + 1)
                    if n >= 2:
                        act.wait_ge(sem("x_stat"), (b + 1) * KT + n - 1)
                    A(TT[n % 2][:, :], XT[:, n, :], ACT.Square).then_inc(sem("x_sq"), 1)

        def ffn_in(f):
            ph = PLAN[f"ffn{f}_in"]

            def step(j, mod=None):
                if mod is not None:
                    act.wait_ge(sem("mod_fold"), j + (MOD_EARLY - 1))
                    mod_rows(j + MOD_EARLY, mod, modrowl[mod])
                slab_wait(ph, j, 0)
                act.wait_ge(sem("hid_ready"), j + (f * FT + 1))
                A(two(TT[0][:, :]), halves(0), ACT.Silu).then_inc(sem("gate_ready"), 1)
                split_hi(ph, j, 0)
                slab_wait(ph, j, 1)
                split_hi(ph, j, 1)
                act.wait_ge(sem("hid_ready"), j + (f * FT + 2))
                A(Mhi[:, bass.ds(j, 1), :], TT[1][:, :].rearrange("p (a b) -> p a b", a=1), ACT.Copy)\
                    .then_inc(sem("mid_hi"), 1)

            if f == 0:
                step(0)
                mod_rows(MOD_EARLY, 0, modrowl[0])
                step(1, 1)
                with act.Fori(1, MOD_LATE // 2) as jj:
                    for s in range(2):
                        step(jj * 2 + s, s)
                with act.Fori(MOD_LATE, FT) as j:
                    step(j)
            else:
                with act.Fori(0, FT) as j:
                    step(j)

        def evac_y(j, n2, y0):
            b = y0 // KT
            act.wait_ge(sem("acc_done"), j * 2 + (y0 + n2 + 1))
            n = j * 2 + n2
            for cond, half, c0, c1 in ((0, 0, 0, CTX), (1, 0, CTX, HALF), (1, 1, 0, HALF)):
                A(Y[:, bass.ds(n, 1), half * HALF + c0:half * HALF + c1], PP[n2][:, half:half + 1, c0:c1], ACT.Copy,
                  scale=Gvec[:, b, bass.ds(n, 1), cond])
            A(two(TT[n2][:, :]), halves(n2), ACT.Square).then_inc(sem("y_sq"), 1)

        def ffn_out(f, y0, last=False):
            ph = PLAN[f"ffn{f}_out"]
            bodies = ph.bodies - 1 if last else ph.bodies
            act.wait_ge(sem("mod_set"), 2)
            with act.Fori(0, bodies) as j:
                for n2 in range(2):
                    for s in range(3):
                        slab_wait(ph, j, 3 * n2 + s)
                        split_hi(ph, j, 3 * n2 + s)
                    evac_y(j, n2, y0)
            if last:
                for n2 in range(2):
                    for s in range(3):
                        slab_wait(ph, bodies, 3 * n2 + s)
                        if 3 * n2 + s < 4:
                            split_hi(ph, bodies, 3 * n2 + s)
                    evac_y(bodies, n2, y0)

        make_h(0)
        ffn_in(0)
        ffn_out(0, 0)
        boundary(0)
        make_h(1)
        act.wait_ge(sem("h_ready"), 2 * KT)
        act.dma_start(maskf[:, :, :], t_mask).then_inc(sem("mask_in"), 16)

        def fourier_re(g):
            act.wait_ge(sem("v_ready"), g + 1)
            pr = 2 * (g % 2)
            A(VRI[g][:, :, 0:P], PP[pr][:, 0, 0:2 * P].rearrange("p (a b) -> p a b", a=2), ACT.Copy)
            A(VRI[g][:, 0, P:T], PP[pr][:, 1, :], ACT.Copy).then_inc(sem("v_re"), 1)

        def fourier_hi(g):
            act.wait_ge(sem("yf_ready"), g + 1)
            A(two(Yhi[:, g, :]), halves(3), ACT.Copy).then_inc(sem("yhi_done"), 1)

        heads = PLAN["mix_heads"]

        def evac_slab(i):
            s = i % 2
            act.wait_ge(slab_done, heads.base + i + 1)
            act.wait_ge(sem("t_free"), i + 1)
            func = ACT.Copy if i >= 5 * NH or i % 5 == 3 else ACT.Sigmoid
            A(two(TT[s][:, :]), halves(s), func).then_inc(sem("t_ready"), 1)
            split_hi(heads, 0, i)

        def level_keys(hd, lev):
            if lev == 1:
                act.wait_ge(sem("ks_ready"), hd + 1)
                if hd:
                    act.wait_ge(sem("lev_mm"), 8 * hd)
            else:
                act.wait_ge(sem("upd_done"), 8 * hd + lev)
                act.wait_ge(sem("lev_mm"), 8 * hd + lev - 1)
            h = 1 << (lev - 1)
            A(KX[lev % 2][:, :].rearrange("p (b e c) -> p b e c", e=2, c=h), level_ap(KD, hd, 0, T, h),
              ACT.Copy).then_inc(sem("kx_ready"), 1)

        def load_states(hd):
            for d in range(2):
                act.dma_start(SV[:, d, 0, :], state_hgrn[0, 0, d, hd]).then_inc(sem("state_in"), 16)

        def token_keys(hd):
            act.wait_ge(sem("kT"), hd + 1)
            for bank in range(2):
                m = A(KTOK[:, 4 * bank:4 * bank + 4, :],
                      PP[pair_of(hd, 0)][:, bank, :].rearrange("p (a b) -> p a b", a=4), ACT.Copy)
            m.then_inc(sem("ktok"), 1)

        def context_states(hd):
            act.wait_ge(sem("kv_mm"), hd + 1)
            if hd:
                act.wait_ge(sem("state_out"), 32 * hd)
            pr = pair_of(hd, 1)
            A(SO[:, :, :], PP[pr][:, :, 0:P], ACT.Copy).then_inc(sem("so_ready"), 1)
            act.wait_ge(sem("so_ready"), hd + 1)
            for d in range(2):
                act.dma_start(new_state[0, 0, d, hd], SO[:, d, :]).then_inc(sem("state_out"), 16)

        def output_square(hd):
            act.wait_ge(sem("o_mm"), hd + 1)
            if hd:
                act.wait_ge(sem("o_done"), hd)
            A(OT[:, :], flat(pair_of(hd, 0))[:, 0:T], ACT.Square).then_inc(sem("o_sq"), 1)
            if hd + 1 < NH:
                load_states(hd + 1)

        def output_std(hd):
            act.wait_ge(sem("o_stat"), hd + 1)
            A(two(OT[:, :]), halves(pair_of(hd, 1)), ACT.Sqrt, bias=EPS).then_inc(sem("o_std"), 1)

        def output_hi(hd):
            act.wait_ge(sem("o_full"), hd + 1)
            A(Ohi[:, hd, :], OT[:, :], ACT.Copy).then_inc(sem("o_hi"), 1)

        load_states(0)
        for h in range(NH + 1):
            if h == NH - 1:
                act.wait_ge(sem("o_done"), 2)
                act.dma_start(DFTS[:, :], t_dft[:, 0:512]).then_inc(sem("dft_in"), 16)
                for part in range(2):
                    for a in range(4):
                        at = 512 + part * 2048 + a * 512
                        act.dma_start(DFTL[part][a][:, :], t_dft[:, at:at + 512]).then_inc(sem("dft_in"), 16)
            if h:
                level_keys(h - 1, 3)
            evac_slab(5 * h)
            if h:
                level_keys(h - 1, 4)
                level_keys(h - 1, 5)
            evac_slab(5 * h + 1)
            if h:
                level_keys(h - 1, 6)
                level_keys(h - 1, 7)
            evac_slab(5 * h + 2)
            if h:
                token_keys(h - 1)
                context_states(h - 1)
            if h < NH:
                level_keys(h, 1)
            evac_slab(5 * h + 3)
            if h:
                output_square(h - 1)
                output_std(h - 1)
            if h < NH:
                act.wait_ge(sem("lev_mm"), 8 * h + 1)
                A(AT[:, :], flat(pair_of(h, 0))[:, 0:T], ACT.Copy).then_inc(sem("at_start"), 1)
            if h:
                output_hi(h - 1)
            if h < NH:
                evac_slab(5 * h + 4)
                level_keys(h, 2)
        act.wait_ge(sem("o_done"), NH)
        for g in range(NH):
            fourier_re(g)
            if g >= 1:
                fourier_hi(g - 1)
        fourier_hi(NH - 1)

        ph = PLAN["mix_merge"]
        with act.Fori(0, ph.bodies) as j:
            for n2 in range(2):
                slab_wait(ph, j, 3 * n2)
                act.wait_ge(sem("mg_ready"), j * 2 + (n2 + 1))
                A(two(TT[0][:, :]), halves(0), ACT.Sigmoid).then_inc(sem("ga_ready"), 1)
                split_hi(ph, j, 3 * n2)
                slab_wait(ph, j, 3 * n2 + 1)
                A(two(TT[1][:, :]), halves(1), ACT.Sigmoid).then_inc(sem("gb_ready"), 1)
                split_hi(ph, j, 3 * n2 + 1)
                slab_wait(ph, j, 3 * n2 + 2)
                split_hi(ph, j, 3 * n2 + 2)
                act.wait_ge(sem("mg_ready"), j * 2 + (n2 + 2))
                A(MGhi[:, bass.ds(j * 2 + n2, 1), :], TT[2][:, :].rearrange("p (a b) -> p a b", a=1), ACT.Copy)\
                    .then_inc(sem("mg_hi"), 1)
        ph = PLAN["mix_out"]
        with act.Fori(0, ph.bodies) as j:
            for s in range(2):
                slab_wait(ph, j, s)
                split_hi(ph, j, s)
                evac_y(j, s, KT)
        boundary(1)
        make_h(2)
        ffn_in(1)
        ffn_out(1, 2 * KT, last=True)
        boundary(2, last=True)

    @block.vector
    def _(dve):
        V = nc.vector

        chain = [0]

        def link(ins):
            chain[0] += 1
            ins.then_inc(sem("dve_chain"), 1)
            dve.wait_ge(sem("dve_chain"), chain[0])

        V.memset(S2[:, :, :], 0.0).then_inc(sem("s2_zero"), 1)
        V.memset(ones_d[:, :], 1.0 / D).then_inc(sem("ones_set"), 1)
        V.memset(ones_h[:, :], 1.0 / P).then_inc(sem("ones_set"), 1)
        V.memset(LB[:, 0, 1:2], 0.0).then_inc(sem("hid_ready"), 1)
        V.memset(LB[:, 0, 6:7], 0.0).then_inc(sem("mid_lo"), 1)
        V.memset(LB[:, 0, 7:8], 0.0).then_inc(sem("mg_done"), 1)
        V.memset(LB[:, 0, 2:3], 0.0).then_inc(sem("mg_ready"), 1)
        V.memset(LB[:, 0, 3:4], 0.0).then_inc(sem("branch_b"), 1)
        V.memset(LB[:, 0, 4:5], 0.0).then_inc(sem("t_free"), 2)
        V.memset(LB[:, 0, 5:6], 0.0).then_inc(sem("acc_done"), 2)
        dve.wait_ge(sem("vec_evac"), 2)
        link(V.tensor_tensor(LB[:, 1, :], VB[:, 4:12], VB[:, 12:20], ALU.max))
        link(V.tensor_tensor(LB[:, 2, :], VB[:, 4:12], LB[:, 1, :], ALU.subtract))
        V.tensor_tensor(LB[:, 3, :], VB[:, 12:20], LB[:, 1, :], ALU.subtract).then_inc(sem("lb_max"), 1)
        dve.wait_ge(sem("lb_exp"), 1)
        link(V.tensor_tensor(LB[:, 1, :], LB[:, 2, :], LB[:, 3, :], ALU.add))
        link(V.reciprocal(LB[:, 3, :], LB[:, 1, :]))
        link(V.tensor_tensor(LB[:, 4, :], LB[:, 2, :], LB[:, 3, :], ALU.mult))
        link(V.tensor_scalar(LB[:, 5, :], LB[:, 4, :], -1.0, 1.0, ALU.mult, ALU.add))

        def mod_vectors(t0, t1):
            for cond in range(2):
                link(V.tensor_tensor(MV[:, t0:t1, cond],
                                     PP[2][:, 0, 2 * t0:2 * t1].rearrange("p (a b) -> p a b", b=2)[:, :, cond],
                                     VA[:, t0:t1], ALU.add))

        def gains(b, pre_part, post_part):
            for cond in range(2):
                sc = MV[:, (3 * b + 1) * KT:(3 * b + 2) * KT, cond]
                gt = MV[:, (3 * b + 2) * KT:(3 * b + 3) * KT, cond]
                pre = VA[:, 72 + b * KT:72 + (b + 1) * KT]
                post = VA[:, 96 + b * KT:96 + (b + 1) * KT]
                if pre_part:
                    link(V.scalar_tensor_tensor(Avec[:, b, :, cond], sc, 1.0, pre, ALU.add, ALU.mult))
                if post_part:
                    link(V.scalar_tensor_tensor(Gvec[:, b, :, cond], gt, 1.0 if b == 1 else 0.5, post,
                                                ALU.mult, ALU.mult))

        def make_h(b):
            dve.wait_ge(sem("x_std"), b + 1)
            link(V.reciprocal(RS[:, :], RS[:, :]))
            if b == 0:
                dve.wait_ge(sem("mod_fold"), MOD_EARLY)
                mod_vectors(0, 2 * KT)
                gains(0, True, False)
                V.memset(LB[:, 0, 0:1], 0.0).then_inc(sem("mod_set"), 1)

            def scaled(n):
                if n >= 3:
                    dve.wait_ge(sem("h_full"), b * KT + n - 2)
                V.tensor_tensor(BT[n % 3][:, :], XT[:, n, :], RS[:, :], ALU.mult).then_inc(sem("h_scaled"), 1)

            for n in range(3):
                scaled(n)
            for n in range(KT):
                dve.wait_ge(sem("h_hi"), b * KT + n + 1)
                V.tensor_tensor(Hlo[:, n, :], BH[n % 3][:, :], Hhi[:, n, :].bitcast(fp32), ALU.subtract)\
                    .then_inc(sem("h_ready"), 1)
                if n + 3 < KT:
                    scaled(n + 3)

        def boundary(b):
            dve.wait_ge(sem("y_std"), b + 1)
            link(V.reciprocal(RS[:, :], RS[:, :]))

            for n in range(KT):
                if n >= 6:
                    dve.wait_ge(sem(f"x_new{n % 2}"), (b * KT + n - 6) // 2 + 1)
                V.tensor_tensor(BT[n % 6][:, :], Y[:, n, :], RS[:, :], ALU.mult).then_inc(sem("y_scaled"), 1)
                if n % 2:
                    dve.wait_ge(sem("y_scaled"), b * KT + n)
                    V.tensor_tensor(XT[:, n - 1, :], XT[:, n - 1, :], BT[(n - 1) % 6][:, :], ALU.add)\
                        .then_inc(sem("x_new0"), 1)

        def ffn_in(f):
            ph = PLAN[f"ffn{f}_in"]

            def step(j):
                dve.wait_ge(slab_done, ph.slab(j, 1) + 1)
                dve.wait_ge(sem("gate_ready"), j + (f * FT + 2))
                dve.wait_ge(sem("mid_hi"), j + (f * FT + 1))
                dve.wait_ge(sem("mid_lo"), j + (f * FT + 1))
                V.tensor_tensor(two(TT[1][:, :]), two(TT[0][:, :]), halves(1), ALU.mult)\
                    .then_inc(sem("hid_ready"), 1)
                dve.wait_ge(sem("mid_hi"), j + (f * FT + 2))
                V.tensor_tensor(Mlo[:, bass.ds(j, 1), :], TT[1][:, :].rearrange("p (a b) -> p a b", a=1),
                                Mhi[:, bass.ds(j, 1), :].bitcast(fp32), ALU.subtract).then_inc(sem("mid_lo"), 1)

            if f == 0:
                with dve.Fori(0, MOD_LATE) as j:
                    step(j)
                dve.wait_ge(sem("mod_fold"), MOD_EARLY + MOD_LATE)
                mod_vectors(2 * KT, NMOD * KT)
                gains(0, False, True)
                gains(1, True, True)
                gains(2, True, True)
                V.memset(LB[:, 1, 0:1], 0.0).then_inc(sem("mod_set"), 1)
                with dve.Fori(MOD_LATE, FT) as j:
                    step(j)
            else:
                with dve.Fori(0, FT) as j:
                    step(j)

        def acc(j, n2, y0):
            dve.wait_ge(sem("y_sq"), j * 2 + (y0 + n2 + 3))
            dve.wait_ge(sem("acc_done"), j * 2 + (y0 + n2 + 2))
            V.tensor_tensor(TT[2][:, :], TT[2][:, :], TT[n2][:, :], ALU.add).then_inc(sem("acc_done"), 1)

        def ffn_out(f, y0, last=False):
            ph = PLAN[f"ffn{f}_out"]
            link(V.memset(TT[2][:, :], 0.0))
            bodies = ph.bodies - 1 if last else ph.bodies
            with dve.Fori(0, bodies) as j:
                for n2 in range(2):
                    acc(j, n2, y0)
            if last:
                for n2 in range(2):
                    acc(bodies, n2, y0)

        make_h(0)
        ffn_in(0)
        ffn_out(0, 0)
        boundary(0)
        make_h(1)

        def fourier_im(g):
            dve.wait_ge(sem("v_ready"), g + 1)
            V.tensor_copy(VRI[g][:, 1, P:T], PP[1][:, g % 2, :]).then_inc(sem("v_im"), 1)

        def fourier_lo(g):
            dve.wait_ge(sem("yhi_done"), g + 1)
            V.tensor_tensor(two(Ylo[:, g, :]), halves(3), two(Yhi[:, g, :]).bitcast(fp32), ALU.subtract)\
                .then_inc(sem("ylo_done"), 1)

        dve.wait_ge(sem("mask_in"), 16)
        V.tensor_copy(mask[:, :, :], maskf[:, :, :]).then_inc(sem("mask_set"), 1)
        dve.wait_ge(sem("mask_set"), 1)

        def blocks(tensor, hd, array, h, side):
            return tensor[:, array, hd, :].rearrange("p (b c) -> p b c", c=2 * h)[:, :, side * h:(side + 1) * h]

        def totals(hd, array, h, side):
            ap = blocks(FD, hd, array, h, side)[:, :, 0:1]
            return ap.to_broadcast([P, T // (2 * h), h]) if h > 1 else ap

        def gated(i, dst):
            dve.wait_ge(sem("t_ready"), i + 1)
            V.tensor_tensor(two(dst), two(TT[i % 2][:, :]), halves(i % 2), ALU.mult).then_inc(sem("t_free"), 1)

        def gate_and_keys(i, d):
            hd = i // 5
            dve.wait_ge(sem("t_ready"), i + 1)
            at = d * NH + hd
            link(V.tensor_scalar(FD[:, 1 - d, hd, :], TT[i % 2][:, :], LB[:, 5, at:at + 1], LB[:, 4, at:at + 1],
                                 ALU.mult, ALU.add))
            V.tensor_scalar(KD[:, d, hd, :], FD[:, 1 - d, hd, :], -1.0, 1.0, ALU.mult, ALU.add)\
                .then_inc(sem("t_free"), 1)
            dve.wait_ge(sem("t_free"), i + 3)

        def token_copy(i, dst):
            dve.wait_ge(sem("tok_T"), i // 5 + 1 if i < 5 * NH else i - 4 * NH + 1)
            V.tensor_copy(dst, flat(i % 2)[:, 0:T].rearrange("p (a b) -> p a b", a=NCH)).then_inc(sem("t_free"), 1)

        def update(hd, lev):
            h = 1 << (lev - 1)
            dve.wait_ge(sem("lev_mm"), 8 * hd + lev + 1)
            dve.wait_ge(sem("upd_done"), 8 * hd + lev)
            V.tensor_tensor(blocks(KD, hd, 0, h, 0), blocks(KD, hd, 0, h, 0), totals(hd, 1, h, 1), ALU.mult)
            V.tensor_tensor(blocks(KD, hd, 1, h, 1), blocks(KD, hd, 1, h, 1), totals(hd, 0, h, 0), ALU.mult)
            V.tensor_tensor(blocks(QD, hd, 0, h, 0), blocks(QD, hd, 0, h, 0), totals(hd, 0, h, 1), ALU.mult)
            link(V.tensor_tensor(blocks(QD, hd, 1, h, 1), blocks(QD, hd, 1, h, 1), totals(hd, 1, h, 0), ALU.mult))
            tot = FD[:, :, hd, :].rearrange("p d (b c) -> p d b c", c=2 * h)
            V.tensor_tensor(tot[:, :, :, 0], tot[:, :, :, 0], tot[:, :, :, h], ALU.mult)\
                .then_inc(sem("upd_done"), 1)
            if lev == 1:
                dve.wait_ge(sem("at_start"), hd + 1)
            else:
                dve.wait_ge(sem("at_done"), 7 * hd + lev - 1)
            V.copy_predicated(AT[:, :].rearrange("p (a b) -> p a b", a=NCH),
                              mask[:, lev - 1:lev, :].to_broadcast([P, NCH, P]),
                              flat(pair_of(hd, lev))[:, 0:T].rearrange("p (a b) -> p a b", a=NCH))\
                .then_inc(sem("at_done"), 1)

        def carry_states(hd):
            dve.wait_ge(sem("state_in"), 32 * (hd + 1))
            dve.wait_ge(sem("so_ready"), hd + 1)
            kv = flat(pair_of(hd, 1))
            for e in range(3):
                V.scalar_tensor_tensor(SV[:, 0, e + 1, :], SV[:, 0, e, :], FD[:, 1, hd, (e + 1) * P:(e + 1) * P + 1],
                                       kv[:, (e + 1) * P:(e + 2) * P], ALU.mult, ALU.add)
                m = V.scalar_tensor_tensor(SV[:, 1, e + 1, :], SV[:, 1, e, :],
                                           FD[:, 0, hd, (4 - e) * P:(4 - e) * P + 1],
                                           kv[:, (7 - e) * P:(8 - e) * P], ALU.mult, ALU.add)
                if e < 2:
                    link(m)
                else:
                    m.then_inc(sem("sv_done"), 1)

        def output_norm(hd):
            dve.wait_ge(sem("o_std"), hd + 1)
            link(V.reciprocal(OT[:, :], OT[:, :]))
            link(V.tensor_tensor(OT[:, :], OT[:, :], flat(pair_of(hd, 0))[:, 0:T], ALU.mult))
            V.scalar_tensor_tensor(OT[:, :], OT[:, :], VB[:, hd:hd + 1], GT[:, hd, :], ALU.mult, ALU.mult)\
                .then_inc(sem("o_full"), 1)

        def output_lo(hd):
            dve.wait_ge(sem("o_hi"), hd + 1)
            V.tensor_tensor(Olo[:, hd, :], OT[:, :], Ohi[:, hd, :].bitcast(fp32), ALU.subtract)\
                .then_inc(sem("o_done"), 1)

        for h in range(NH + 1):
            if h:
                update(h - 1, 1)
                gated(5 * h - 1, GT[:, h - 1, :])
                update(h - 1, 2)
                update(h - 1, 3)
            if h < NH:
                gated(5 * h, QD[:, 0, h, :])
            if h:
                update(h - 1, 4)
            if h == NH:
                token_copy(5 * NH, UT[0][:, :, :])
            if h:
                update(h - 1, 5)
            if h < NH:
                gate_and_keys(5 * h + 1, 0)
                link(V.tensor_tensor(QD[:, 1, h, :], QD[:, 0, h, :], FD[:, 1, h, :], ALU.mult))
            if h:
                update(h - 1, 6)
            if h == NH:
                token_copy(5 * NH + 1, UT[1][:, :, :])
            if h:
                update(h - 1, 7)
            if h < NH:
                gate_and_keys(5 * h + 2, 1)
                V.tensor_tensor(KX[0][:, :], KD[:, 0, h, :], KD[:, 1, h, :], ALU.add).then_inc(sem("ks_ready"), 1)
            if h:
                carry_states(h - 1)
            if h == NH:
                token_copy(5 * NH + 2, UT[2][:, :, :])
            if h:
                output_norm(h - 1)
            if h < NH:
                dve.wait_ge(sem("lev_mm"), 8 * h + 1)
                V.tensor_tensor(QD[:, 0, h, :], QD[:, 0, h, :], FD[:, 0, h, :], ALU.mult).then_inc(sem("upd_done"), 1)
            if h:
                output_lo(h - 1)
            if h < NH:
                token_copy(5 * h + 3, VT[:, :, h * P:(h + 1) * P])
        token_copy(5 * NH + 3, UT[3][:, :, :])
        for g in range(NH):
            fourier_im(g)
            if g >= 1:
                fourier_lo(g - 1)
        fourier_lo(NH - 1)

        ph = PLAN["mix_merge"]
        with dve.Fori(0, ph.bodies) as j:
            for n2 in range(2):
                dve.wait_ge(slab_done, ph.slab(j, 3 * n2 + 2) + 1)
                dve.wait_ge(sem("gb_ready"), j * 2 + (n2 + 2))
                V.tensor_tensor(two(TT[0][:, :]), two(TT[0][:, :]), halves(2), ALU.mult).then_inc(sem("branch_a"), 1)
                V.tensor_tensor(two(TT[1][:, :]), two(TT[1][:, :]), halves(3), ALU.mult).then_inc(sem("branch_b"), 1)
                dve.wait_ge(sem("branch_a"), j * 2 + (n2 + 1))
                dve.wait_ge(sem("branch_b"), j * 2 + (n2 + 2))
                dve.wait_ge(sem("mg_done"), j * 2 + (n2 + 1))
                V.tensor_tensor(TT[2][:, :], TT[0][:, :], TT[1][:, :], ALU.add).then_inc(sem("mg_ready"), 1)
                dve.wait_ge(sem("mg_hi"), j * 2 + (n2 + 1))
                V.tensor_tensor(MGlo[:, bass.ds(j * 2 + n2, 1), :], TT[2][:, :].rearrange("p (a b) -> p a b", a=1),
                                MGhi[:, bass.ds(j * 2 + n2, 1), :].bitcast(fp32), ALU.subtract)\
                    .then_inc(sem("mg_done"), 1)
        ph = PLAN["mix_out"]
        dve.wait_ge(sem("mg_done"), KT + 1)
        link(V.memset(TT[2][:, :], 0.0))
        with dve.Fori(0, ph.bodies) as j:
            for s in range(2):
                acc(j, s, KT)
        dve.wait_ge(sem("state_out"), 32 * NH)
        boundary(1)
        make_h(2)
        ffn_in(1)
        ffn_out(1, 2 * KT, last=True)
        boundary(2)

    block_cm.__exit__(None, None, None)


_INS = ["x_prompt", "x_sample", "state_hgrn", "c", "c_ctx", "w_mod", "b_mod", "norm_pre", "norm_post", "ffn_w_in",
        "ffn_w_out", "w_in", "w_four", "hgrn_gain", "w_hgrn", "w_out", "lb_logits"]
_OUTS = [(1, 128, 1024), (1, 512, 1024), (1, 1, 2, 4, 128, 128)]


def _tables():
    import numpy as np

    n = np.arange(P)
    const = np.zeros((P, P + 2), np.float32)
    const[n, n] = 1.0
    for q in range(4):
        for r in range(2):
            const[32 * q + r, P + r] = 1.0
    turn = 2 * np.pi * (np.outer(n, n) % P) / P
    t = np.arange(LAT)
    row, col = t // 64, t % 64
    turn_lat = 2 * np.pi * ((8 * (row[:, None] * row[None, :] % 8) + col[:, None] * col[None, :] % 64) % 64) / 64
    lat = [f(turn_lat).reshape(4, P, LAT).transpose(1, 0, 2).reshape(P, 4 * LAT) / 256 for f in (np.cos, np.sin)]
    dft = np.concatenate([np.cos(turn), -np.sin(turn), np.cos(turn) / P, np.sin(turn) / P] + lat, axis=1)
    x = n[:, None] ^ n[None, :]
    mask = np.stack([(x >> k) == 1 for k in range(7)], axis=1)
    return {"t_const": const, "t_dft": dft.astype(np.float32), "t_mask": mask.astype(np.float32)}


def kernel(**inputs):
    import numpy as _np
    import concourse.bacc as _bacc
    from concourse import mybir as _mybir
    from concourse.bass_utils import run_bass_kernel_spmd as _run

    nc = _bacc.Bacc("TRN2", target_bir_lowering=False, num_devices=1)
    arrays, args = {}, []
    feed = [(name, _np.ascontiguousarray(inputs[name])) for name in _INS] + list(_tables().items())
    for name, a in feed:
        arrays[f"in_{name}"] = a
        args.append(nc.dram_tensor(f"in_{name}", a.shape, _mybir.dt.from_np(a.dtype), kind="ExternalInput").ap())
    for i, shape in enumerate(_OUTS):
        args.append(nc.dram_tensor(f"out_{i}", shape, _mybir.dt.float32, kind="ExternalOutput").ap())
    hybrid_step_kernel(nc, *args)
    r = _run(nc, [arrays], core_ids=[0])
    return tuple(r.results[0][f"out_{i}"] for i in range(len(_OUTS)))
```

```python
import concourse.bass as bass
from concourse import mybir

P = 128
D = 1024
KT = D // P
CTX, LAT = 128, 512
T = CTX + LAT
HALF = T // 2
QT = T // 4
NCH = T // P
DFF = 2816
FT = DFF // P
NH = 4
NMOD = 9
EPS = 1e-6
TB = T * 4
W_IN_GATES = 3072

fp32 = mybir.dt.float32
fp32r = mybir.dt.float32r
u8 = mybir.dt.uint8
ACT = mybir.ActivationFunctionType
ALU = mybir.AluOpType

PHASES = [
    ("ffn0_in", FT, [1, 1]),
    ("ffn0_out", KT // 2, [1] * 6),
    ("mix_heads", NH // 2, [1] * 10),
    ("mix_u", NH // 2, [1, 1]),
    ("mix_merge", KT // 2, [1, 1, 2, 1, 1, 2]),
    ("mix_out", KT // 2, [1, 1]),
    ("ffn1_in", FT, [1, 1]),
    ("ffn1_out", KT // 2, [1] * 6),
]
MOD_EARLY = 4
MOD_LATE = NMOD * D // 512 - MOD_EARLY
MOD_AFTER = (4, 5, 7, None)
MOD_LATE_FREE = MOD_LATE
HEAD_COLS = [512, 1024, 1536, 2048, 2560]
KEYS = [(0, 0), (0, 1), (0, 2), (0, 3), (1, 0), (1, 2), (1, 3), (1, 4)]
OUT_SPLIT = [(0, 8), (8, 7), (15, 7)]


class Phase:

    def __init__(self, slabs, dmas, bodies, kinds):
        self.base, self.raw0, self.bodies, self.kinds = slabs, list(dmas), bodies, kinds
        self.per = len(kinds)
        self.raw_per = [16 * sum(k for n, k in enumerate(kinds) if n % 2 == s) for s in (0, 1)]

    def slab(self, body, pos):
        return body * self.per + (self.base + pos)

    def raw_need(self, body, pos):
        body, pos = body + pos // self.per, pos % self.per
        s = pos % 2
        within = 16 * sum(k for n, k in enumerate(self.kinds[:pos + 1]) if n % 2 == s)
        return body * self.raw_per[s] + (self.raw0[s] + within)


def plan():
    out, slabs, dmas = {}, 0, [0, 0]
    for name, bodies, kinds in PHASES:
        ph = Phase(slabs, dmas, bodies, kinds)
        out[name] = ph
        slabs += bodies * ph.per
        dmas = [dmas[s] + bodies * ph.raw_per[s] for s in (0, 1)]
    return out, slabs


def hybrid_step_kernel(nc, x_prompt, x_sample, state_hgrn, c, c_ctx, w_mod, b_mod, norm_pre, norm_post,
                       ffn_w_in, ffn_w_out, w_in, w_four, hgrn_gain, w_hgrn, w_out, lb_logits,
                       t_const, t_dft, t_mask, y_prompt, y_sample, new_state):
    PLAN, NSLAB = plan()

    top = [(nc.sbuf_base + 31) // 32 * 32]

    def place(name, shape, dtype, at=None):
        size = mybir.dt.size(dtype)
        for n in shape[1:]:
            size *= n
        if at is None:
            at = top[0]
            top[0] = (at + size + 31) // 32 * 32
        return nc.alloc_sbuf_tensor_at(name, shape, dtype, offset=at)

    XT = place("XT", [P, KT, T], fp32)
    h_at = top[0]
    Hhi = place("Hhi", [P, KT, T], fp32r)
    Hlo = place("Hlo", [P, KT, T], fp32r)
    Y = place("Y", [P, KT, T], fp32, at=h_at)
    mid_at = top[0]
    Mhi = place("Mhi", [P, FT, T], fp32r)
    Mlo = place("Mlo", [P, FT, T], fp32r)
    raw = [place(f"raw{s}", [P, KT, P], fp32) for s in (0, 1)]
    Whi = [place(f"Whi{s}", [P, KT, P], fp32r) for s in (0, 1)]
    Wlo = [place(f"Wlo{s}", [P, KT, P], fp32r) for s in (0, 1)]
    TT = [place(f"TT{s}", [P, T], fp32) for s in (0, 1, 2)]
    ident = place("ident", [P, P + 32], fp32)
    ones_d = place("ones_d", [P, P], fp32)
    SEL = place("SEL", [P, 4, P], fp32)
    RQ = place("RQ", [P, QT], fp32)
    VA = place("VA", [P, 120], fp32)
    VB = place("VB", [P, 36], fp32)
    MV = place("MV", [P, NMOD * KT, 2], fp32)
    Avec = place("Avec", [P, 3, KT, 2], fp32)
    Gvec = place("Gvec", [P, 3, KT, 2], fp32)
    LB = place("LB", [P, 5, 8], fp32)
    mask = place("mask", [P, 7, P], u8)
    assert top[0] <= nc.sbuf_usable_end, (top[0], nc.sbuf_usable_end)

    def tile_at(n):
        return mid_at + n * TB

    xtok = place("xtok", [P, NCH, D], fp32, at=tile_at(0))
    rowsA = place("rowsA", [120, P], fp32, at=tile_at(8))
    rowsB = place("rowsB", [36, P], fp32, at=tile_at(8) + 512)
    modrow = place("modrow", [P, 512], fp32, at=tile_at(9))
    spare = place("spare", [P, 8], fp32, at=tile_at(10))
    modw = [place(f"modw{s}", [P, KT, 512], fp32, at=tile_at(11) + 16384 * s) for s in range(4)]
    late_at = [tile_at(MOD_LATE_FREE), tile_at(FT + MOD_LATE_FREE)]
    modl = [place(f"modl{s}", [P, KT, 512], fp32, at=late_at[s]) for s in (0, 1)]
    modrowl = place("modrowl", [P, 512], fp32, at=late_at[0] + 16384)
    SW = [place(f"SW{s}", [P, KT, 32], fp32, at=late_at[1] + 16384 + 1024 * s) for s in (0, 1)]
    S2 = place("S2", [P, KT, 62], fp32, at=late_at[1] + 16384 + 2048)
    BT = [place(f"BT{s}", [P, T], fp32, at=tile_at(n)) for s, n in enumerate((37, 38, 39, 40, 41, 42))]
    BH = BT[3:6]
    OUTB = place("OUTB", [P, NCH, D], fp32, at=tile_at(0))
    Yhi = place("Yhi", [P, NH, T], fp32r, at=tile_at(0))
    Ylo = place("Ylo", [P, NH, T], fp32r, at=tile_at(4))
    UT = [place(f"UT{g}", [P, NCH, P], fp32, at=tile_at(18 + 4 * g)) for g in range(NH)]
    VRI = [place(f"VRI{g}", [P, 2, T], fp32, at=tile_at(n)) for g, n in enumerate((32, 34, 37, 40))]
    DFTS = place("DFTS", [P, 512], fp32, at=tile_at(36))
    DFTL = [[place(f"DFTL{part}{a}", [P, 512], fp32, at=tile_at(16 + 8 * part + 4 * (a // 2) + a % 2))
             for a in range(4)] for part in range(2)]
    QD = place("QD", [P, 2, NH, T], fp32, at=tile_at(8))
    KD = place("KD", [P, 2, NH, T], fp32, at=tile_at(16))
    FD = place("FD", [P, 2, NH, T], fp32, at=tile_at(24))
    VT = place("VT", [P, NCH, 512], fp32, at=tile_at(32))
    GT = place("GT", [P, NH, T], fp32, at=tile_at(36))
    AT = place("AT", [P, T], fp32, at=tile_at(0))
    KX = [place(f"KX{n}", [P, T], fp32, at=tile_at(1 + n)) for n in range(2)]
    OSQ = place("OSQ", [P, T], fp32, at=tile_at(3))
    OT = place("OT", [P, T], fp32, at=tile_at(7))
    maskf = place("maskf", [P, 7, P], fp32, at=tile_at(4))
    KTOK = place("KTOK", [P, 8, P], fp32, at=tile_at(40))
    SV = place("SV", [P, 2, 4, P], fp32, at=tile_at(40) + 4096)
    SO = place("SO", [P, 2, P], fp32, at=tile_at(40) + 8192)
    Ohi = place("Ohi", [P, NH, T], fp32r, at=tile_at(8))
    Olo = place("Olo", [P, NH, T], fp32r, at=tile_at(12))
    MGhi = place("MGhi", [P, KT, T], fp32r, at=tile_at(16))
    MGlo = place("MGlo", [P, KT, T], fp32r, at=tile_at(24))

    PP = [nc.alloc_psum_tensor(f"PP{n}", [P, 2, 512], fp32) for n in range(4)]

    def halves(n):
        return PP[n][:, :, 0:HALF]

    def flat(n):
        return PP[n][:, :, :].rearrange("p a b -> p (a b)")

    def two(ap):
        return ap.rearrange("p (a b) -> p a b", a=2)

    sems = {}

    def sem(name):
        if name not in sems:
            sems[name] = nc.alloc_semaphore(name)
        return sems[name]

    raw_full = [sem("raw_full0"), sem("raw_full1")]
    hi_done, lo_done = sem("hi_done"), sem("lo_done")
    slab_done = sem("slab_done")

    TOK = [(0, 0, CTX), (1, CTX, T)]

    def level_ap(tensor, hd, first, tokens, h):
        base = tensor[:, 0, hd, first:first + tokens]
        return bass.AP(base.tensor, base.offset,
                       [[2 * NH * T, P], [2 * h, tokens // (2 * h)], [NH * T + h, 2], [1, h]])

    POOL_TILES = (0, 2, 3, 5)

    def x_new_need(b, n):
        if n in POOL_TILES:
            return sem("x_new_pool"), b * len(POOL_TILES) + POOL_TILES.index(n) + 1
        others = [m for m in range(KT) if m not in POOL_TILES]
        return sem("x_new_dve"), b * len(others) + others.index(n) + 1

    def pair_of(hd, lev):
        return 2 + (hd + lev) % 2

    block_cm = nc.Block()
    block = block_cm.__enter__()

    @block.sync
    def _(sp):
        sp.dma_start(ident[:, :], t_const).then_inc(sem("const_in"), 16)
        sp.dma_start(rowsA[0:72, :], b_mod.rearrange("l (r q) -> (l r) q", q=P)).then_inc(sem("rows_in"), 16)
        sp.dma_start(rowsA[72:96, :], norm_pre.rearrange("l s (r q) -> (l s r) q", q=P)).then_inc(sem("rows_in"), 16)
        sp.dma_start(rowsA[96:120, :], norm_post.rearrange("l s (r q) -> (l s r) q", q=P)).then_inc(sem("rows_in"), 16)
        sp.dma_start(rowsB[0:4, :], hgrn_gain.rearrange("l (r q) -> (l r) q", q=P)).then_inc(sem("rows_in"), 16)
        sp.dma_start(rowsB[4:20, :], lb_logits.rearrange("l d (r q) -> (l d r) q", q=P)).then_inc(sem("rows_in"), 16)
        sp.dma_start(rowsB[20:28, :], c.rearrange("l (r q) -> (l r) q", q=P)).then_inc(sem("rows_in"), 16)
        sp.dma_start(rowsB[28:36, :], c_ctx.rearrange("(r q) -> r q", q=P)).then_inc(sem("rows_in"), 16)
        sp.dma_start(xtok[:, 0, :], x_prompt[0]).then_inc(sem("x_in"), 16)
        sp.dma_start(xtok[:, 1:NCH, :], x_sample[0].rearrange("(a p) f -> p a f", p=P)).then_inc(sem("x_in"), 16)
        wm = w_mod[0].rearrange("(k p) n -> p k n", p=P)
        for i in range(MOD_EARLY):
            sp.dma_start(modw[i][:, :, :], wm[:, :, i * 512:(i + 1) * 512]).then_inc(sem(f"modw_in{i}"), 16)

        def load(ph, body, pos, parts, first=False):
            if not first:
                sp.wait_ge(lo_done, ph.slab(body, pos) - 1)
            for k0, kn, src in parts:
                sp.dma_start(raw[pos % 2][:, k0:k0 + kn, :], src).then_inc(raw_full[pos % 2], 16)

        def col(ap, start):
            return ap[:, :, bass.ds(start, P)]

        def ffn_in_pair(ph, w, j, first=False):
            load(ph, j, 0, [(0, KT, col(w, j * P))], first)
            load(ph, j, 1, [(0, KT, col(w, j * P + DFF))], first)

        def load_mod(i, s):
            sp.dma_start(modl[s][:, :, :], wm[:, :, bass.ds(i * 512, 512)]).then_inc(sem(f"modl_in{s}"), 16)

        def load_ffn_in(f):
            ph = PLAN[f"ffn{f}_in"]
            w = ffn_w_in[0, f].rearrange("(k p) n -> p k n", p=P)
            if f == 0:
                ffn_in_pair(ph, w, 0, first=True)
                sp.wait_ge(sem("mod_mm"), MOD_EARLY)
                load_mod(MOD_EARLY, 0)
                ffn_in_pair(ph, w, 1)
                sp.wait_ge(sem("h_ready"), KT)
                load_mod(MOD_EARLY + 1, 1)
                with sp.Fori(0, MOD_LATE // 2 - 1) as jj:
                    for s in range(2):
                        ffn_in_pair(ph, w, jj * 2 + (2 + s))
                        sp.wait_ge(sem("mod_mm"), jj * 2 + (MOD_EARLY + s + 1))
                        load_mod(jj * 2 + (MOD_EARLY + 2 + s), s)
                with sp.Fori(MOD_LATE, FT) as j:
                    ffn_in_pair(ph, w, j)
            else:
                with sp.Fori(0, FT) as j:
                    ffn_in_pair(ph, w, j)

        def load_ffn_out(f):
            ph = PLAN[f"ffn{f}_out"]
            w = ffn_w_out[0, f].rearrange("(k p) n -> p k n", p=P)
            with sp.Fori(0, ph.bodies) as j:
                for n2 in range(2):
                    for s, (k0, kn) in enumerate(OUT_SPLIT):
                        load(ph, j, 3 * n2 + s, [(0, kn, w[:, k0:k0 + kn, bass.ds(j * 2 * P + n2 * P, P)])])

        load_ffn_in(0)
        load_ffn_out(0)
        wi = w_in[0].rearrange("(k p) n -> p k n", p=P)
        ph = PLAN["mix_heads"]
        with sp.Fori(0, ph.bodies) as hp:
            for a in range(2):
                for n, first_col in enumerate(HEAD_COLS):
                    load(ph, hp, 5 * a + n, [(0, KT, col(wi, hp * 2 * P + (first_col + a * P)))])
        ph = PLAN["mix_u"]
        with sp.Fori(0, ph.bodies) as j:
            for s in range(2):
                load(ph, j, s, [(0, KT, col(wi, j * 2 * P + s * P))])
        ph = PLAN["mix_merge"]
        w4 = w_four[0].rearrange("(k p) n -> p k n", p=P)
        wh = w_hgrn[0].rearrange("(k p) n -> p k n", p=P)
        with sp.Fori(0, ph.bodies) as j:
            for n2 in range(2):
                at = j * 2 * P + n2 * P
                load(ph, j, 3 * n2, [(0, KT, col(wi, at + W_IN_GATES))])
                load(ph, j, 3 * n2 + 1, [(0, KT, col(wi, at + (W_IN_GATES + D)))])
                load(ph, j, 3 * n2 + 2, [(0, NH, col(w4, (j * P + n2 * (P // 2)) * 2)), (NH, NH, col(wh, at))])
        ph = PLAN["mix_out"]
        wo = w_out[0].rearrange("(k p) n -> p k n", p=P)
        with sp.Fori(0, ph.bodies) as j:
            for s in range(2):
                load(ph, j, s, [(0, KT, col(wo, j * 2 * P + s * P))])
        load_ffn_in(1)
        load_ffn_out(1)
        for part in range(KT // 2):
            sp.wait_ge(sem("out_tile"), 2 * (part + 1))
            cols = slice(2 * P * part, 2 * P * (part + 1))
            sp.dma_start(y_prompt[0][:, cols], OUTB[:, 0, cols]).then_inc(sem("y_out"), 16)
            sp.dma_start(y_sample[0].rearrange("(a p) f -> p a f", p=P)[:, :, cols],
                         OUTB[:, 1:NCH, cols]).then_inc(sem("y_out"), 16)
        sp.wait_ge(sem("y_out"), 16 * KT)


    @block.gpsimd
    def _(pool):
        def split_lo(first, count):
            with pool.Fori(0, count // 2) as j:
                for s in range(2):
                    pool.wait_ge(hi_done, j * 2 + (first + s + 1))
                    nc.gpsimd.tensor_tensor(Wlo[s][:, :, :], raw[s][:, :, :], Whi[s][:, :, :].bitcast(fp32),
                                            ALU.subtract).then_inc(lo_done, 1)

        def boundary(b):
            for n in POOL_TILES:
                pool.wait_ge(sem("y_scaled"), b * KT + n + 1)
                nc.gpsimd.tensor_tensor(XT[:, n, :], XT[:, n, :], BT[n % 6][:, :], ALU.add)\
                    .then_inc(sem("x_new_pool"), 1)

        first = 0
        for b, name in enumerate(("mix_heads", "ffn1_in", None)):
            until = PLAN[name].base + 2 if name else NSLAB
            split_lo(first, until - first)
            boundary(b)
            first = until
    @block.tensor
    def _(pe):
        mm = nc.tensor.matmul

        def slab(ph, body, pos, rhs, outs, first_slab=True, last_slab=True, ready=None):
            pe.wait_ge(lo_done, ph.slab(body, pos) + 1)
            s = pos % 2
            count = {}
            last = None
            for k, ((hi, lo), out) in enumerate(zip(rhs, outs)):
                if ready:
                    pe.wait_ge(sem(ready[0]), ready[1] + k + 1)
                n = outs.count(out)
                seen = count.get(out, 0)
                count[out] = seen + 1
                for a, (w, x) in enumerate(((Whi[s], hi), (Whi[s], lo), (Wlo[s], hi))):
                    for half in range(2):
                        last = mm(PP[out][:, half, 0:HALF], w[:, k, :], x[:, half * HALF:(half + 1) * HALF],
                                  start=first_slab and seen == 0 and a == 0,
                                  stop=last_slab and seen == n - 1 and a == 2)
            last.then_inc(slab_done, 1)

        def first_slabs(ph, b):
            for s in range(2):
                pe.wait_ge(lo_done, ph.slab(0, s) + 1)
            order = [(s, k) for k in range(KT // 2) for s in range(2)]
            order += [(s, k) for s in range(2) for k in range(KT // 2, KT)]
            for s, k in order:
                if s == 0:
                    pe.wait_ge(sem("h_ready"), b * KT + k + 1)
                hi, lo = h_tiles[k]
                for a, (w, x) in enumerate(((Whi[s], hi), (Whi[s], lo), (Wlo[s], hi))):
                    for half in range(2):
                        m = mm(PP[s][:, half, 0:HALF], w[:, k, :], x[:, half * HALF:(half + 1) * HALF],
                               start=k == 0 and a == 0, stop=k == KT - 1 and a == 2)
                if k == KT - 1:
                    m.then_inc(slab_done, 1)

        h_tiles = [(Hhi[:, k, :], Hlo[:, k, :]) for k in range(KT)]

        def stat(src, pr, one, first=True, last=True):
            for q in range(4):
                m = mm(PP[pr][32 * q:32 * q + 32, 0, 0:QT], one[:, 0:32], src[:, q * QT:(q + 1) * QT],
                       start=first, stop=last)
            return m

        def spread(pr):
            for q in range(4):
                at = q % 2 * QT
                m = mm(PP[pr][:, q // 2, at:at + QT], SEL[:, q, :], RQ[:, :], start=True, stop=True)
            return m

        def spread_x(b):
            pe.wait_ge(sem("x_rstd"), b + 1)
            spread(2).then_inc(sem("x_spread"), 1)

        def transpose(out, in_):
            k = in_.shape[0]
            return nc.tensor.transpose(out, in_, ident[0:k, 0:k])

        pe.wait_ge(sem("const_in"), 16)
        pe.wait_ge(sem("rows_in"), 16 * 7)
        transpose(PP[2][:, 0, 0:120], rowsA[:, :]).then_inc(sem("vec_T"), 1)
        transpose(PP[2][:, 1, 0:36], rowsB[:, :]).then_inc(sem("vec_T"), 1)
        pe.wait_ge(sem("x_in"), 32)
        pe.wait_ge(sem("ones_set"), 2)

        def mod_slab(w, vec, first=False):
            for k in range(KT):
                q = k % 4
                m = mm(PP[3][32 * q:32 * q + 32, 0, :], vec(k), w[:, k, :], start=first and k < 4,
                       stop=k >= 4, skip_group_check=not first)
            m.then_inc(sem("mod_mm"), 1)

        def early_mod(i):
            pe.wait_ge(sem(f"modw_in{i}"), 16)
            pe.wait_ge(sem("silu_c"), 2)
            mod_slab(modw[i], lambda k: S2[:, k, 30 - 2 * i:62 - 2 * i], i == 0)

        def fold_mod(i, rows):
            pe.wait_ge(sem("modrow"), i + 1)
            for q in range(4):
                at = i * P + q * 32
                m = mm(PP[3][:, 1, at:at + 32], rows[:, q * P:(q + 1) * P], ident[:, P:P + 32],
                       start=True, stop=True)
            m.then_inc(sem("mod_fold"), 1)

        for n in range(KT):
            if n >= 2:
                pe.wait_ge(sem("x_sq"), n - 1)
            for ch in range(NCH):
                m = transpose(flat(n % 2)[:, ch * P:(ch + 1) * P], xtok[:, ch, n * P:(n + 1) * P])
            m.then_inc(sem("x_T"), 1)
            if n >= 1:
                pe.wait_ge(sem("x_sq"), n)
                stat(TT[(n - 1) % 2], 2, ones_d, n == 1, False).then_inc(sem("x_stat"), 1)
            if n in MOD_AFTER:
                early_mod(MOD_AFTER.index(n))
        pe.wait_ge(sem("x_sq"), KT)
        stat(TT[(KT - 1) % 2], 2, ones_d, False, True).then_inc(sem("x_stat"), 1)
        early_mod(MOD_EARLY - 1)
        spread_x(0)
        fold_mod(0, modrow)

        def ffn_in(f):
            ph = PLAN[f"ffn{f}_in"]

            def step(j, mod=None, first=False):
                if mod is not None:
                    jj, s = mod
                    pe.wait_ge(sem(f"modl_in{s}"), jj * 16 + 16)
                    pe.wait_ge(sem("sw_set"), j + 1)
                    mod_slab(modl[s], lambda k: SW[s][:, k, :], first)
                if first:
                    return
                pe.wait_ge(sem("gate_ready"), j + (f * FT + 1))
                slab(ph, j, 0, h_tiles, [0] * KT)
                pe.wait_ge(sem("hid_ready"), j + (f * FT + 1))
                slab(ph, j, 1, h_tiles, [1] * KT)

            first_slabs(ph, 2 * f)
            if f == 0:
                pe.wait_ge(sem("modrow"), 1)
                step(0, (0, 0), first=True)
                step(1, (0, 1))
                with pe.Fori(1, MOD_LATE // 2) as jj:
                    for s in range(2):
                        step(jj * 2 + s, (jj, s))
                step(MOD_LATE)
                fold_mod(1, modrowl)
                with pe.Fori(MOD_LATE + 1, FT) as j:
                    step(j)
            else:
                with pe.Fori(1, FT) as j:
                    step(j)

        def ffn_out(f, y0):
            ph = PLAN[f"ffn{f}_out"]
            pe.wait_ge(sem("gate_ready"), (f + 1) * FT + 1)
            with pe.Fori(0, ph.bodies) as j:
                for n2 in range(2):
                    pe.wait_ge(sem("y_sq"), j * 2 + (y0 + n2 + 1))
                    for s, (k0, kn) in enumerate(OUT_SPLIT):
                        pe.wait_ge(sem("mid_lo"), f * FT + k0 + kn + 1)
                        slab(ph, j, 3 * n2 + s, [(Mhi[:, k, :], Mlo[:, k, :]) for k in range(k0, k0 + kn)],
                             [n2] * kn, first_slab=s == 0, last_slab=s == 2)

        def boundary(b, y0, last=False):
            pe.wait_ge(sem("acc_done"), y0 + KT + 2)
            stat(TT[2], 3, ones_d).then_inc(sem("y_stat"), 1)
            pe.wait_ge(sem("y_rstd"), b + 1)
            spread(3).then_inc(sem("y_spread"), 1)
            if last:
                for n in range(KT):
                    pe.wait_ge(*x_new_need(b, n))
                    if n >= 2:
                        pe.wait_ge(sem("out_tile"), n - 1)
                    for ch in range(NCH):
                        m = transpose(flat(n % 2)[:, ch * P:(ch + 1) * P], XT[:, n, ch * P:(ch + 1) * P])
                    m.then_inc(sem("out_T"), 1)
                return
            for n in range(KT):
                pe.wait_ge(sem("x_sq"), (b + 1) * KT + n + 1)
                stat(TT[n % 2], 2, ones_d, n == 0, n == KT - 1).then_inc(sem("x_stat"), 1)
            spread_x(b + 1)

        ffn_in(0)
        ffn_out(0, 0)
        boundary(0, 0)

        heads, first = PLAN["mix_heads"], PLAN["mix_heads"].base

        def quarter(i, part):
            s = i % 2
            if part == 0:
                pe.wait_ge(lo_done, first + i + 1)
                pe.wait_ge(sem("t_free"), i + 1)
            for k in (2 * part, 2 * part + 1):
                hi, lo = h_tiles[k]
                for a, (w, x) in enumerate(((Whi[s], hi), (Whi[s], lo), (Wlo[s], hi))):
                    for half in range(2):
                        m = mm(PP[s][:, half, 0:HALF], w[:, k, :], x[:, half * HALF:(half + 1) * HALF],
                               start=k == 0 and a == 0, stop=k == KT - 1 and a == 2)
            if part == 3:
                m.then_inc(slab_done, 1)

        def token_major(i):
            s = i % 2
            pe.wait_ge(sem("t_ready"), i + 1)
            for ch in range(NCH):
                m = transpose(flat(s)[:, ch * P:(ch + 1) * P], TT[s][:, ch * P:(ch + 1) * P])
            m.then_inc(sem("tok_T"), 1)

        def diagonal(hd):
            pe.wait_ge(sem("ks_ready"), hd + 1)
            if hd:
                pe.wait_ge(sem("o_std"), hd)
            for ch in range(NCH):
                cols = slice(ch * P, (ch + 1) * P)
                m = mm(flat(pair_of(hd, 0))[:, cols], KX[0][:, cols], QD[:, 0, hd, cols], start=True, stop=True)
            m.then_inc(sem("lev_mm"), 1)

        def level(hd, lev):
            pe.wait_ge(sem("kx_ready"), 7 * hd + lev)
            pe.wait_ge(sem("upd_done"), 8 * hd + lev)
            if lev == 1:
                if hd:
                    pe.wait_ge(sem("o_full"), hd)
            elif lev == 2:
                pe.wait_ge(sem("at_start"), hd + 1)
            else:
                pe.wait_ge(sem("at_done"), 7 * hd + lev - 2)
            for ch in range(NCH):
                m = mm(flat(pair_of(hd, lev))[:, ch * P:(ch + 1) * P], KX[lev % 2][:, ch * P:(ch + 1) * P],
                       level_ap(QD, hd, ch * P, P, 1 << (lev - 1)), start=True, stop=True)
            m.then_inc(sem("lev_mm"), 1)

        def keys_to_tokens(hd):
            pe.wait_ge(sem("upd_done"), 8 * hd + 8)
            pe.wait_ge(sem("at_done"), 7 * hd + 6)
            for e, (d, ch) in enumerate(KEYS):
                m = transpose(flat(pair_of(hd, 0))[:, e * P:(e + 1) * P], KD[:, d, hd, ch * P:(ch + 1) * P])
            m.then_inc(sem("kT"), 1)

        def key_values(hd):
            pe.wait_ge(sem("ktok"), hd + 1)
            pe.wait_ge(sem("t_free"), 5 * hd + 4 + 2)
            pe.wait_ge(sem("at_done"), 7 * hd + 7)
            for e, (d, ch) in enumerate(KEYS):
                m = mm(flat(pair_of(hd, 1))[:, e * P:(e + 1) * P], KTOK[:, e, :], VT[:, ch, hd * P:(hd + 1) * P],
                       start=True, stop=True)
            m.then_inc(sem("kv_mm"), 1)

        def outputs(hd):
            pe.wait_ge(sem("sv_done"), hd + 1)
            for ch in range(NCH):
                out = flat(pair_of(hd, 0))[:, ch * P:(ch + 1) * P]
                m = mm(out, VT[:, ch, hd * P:(hd + 1) * P], AT[:, ch * P:(ch + 1) * P], start=True, stop=ch == 0)
                if ch:
                    mm(out, SV[:, 0, ch - 1, :], QD[:, 1, hd, ch * P:(ch + 1) * P], start=False, stop=False)
                    m = mm(out, SV[:, 1, 4 - ch, :], QD[:, 0, hd, ch * P:(ch + 1) * P], start=False, stop=True)
            m.then_inc(sem("o_mm"), 1)

        def output_stat(hd):
            pe.wait_ge(sem("o_sq"), hd + 1)
            stat(OSQ, pair_of(hd, 1), ones_d).then_inc(sem("o_stat"), 1)

        def output_spread(hd):
            pe.wait_ge(sem("o_rstd"), hd + 1)
            spread(pair_of(hd, 0)).then_inc(sem("o_spread"), 1)

        first_slabs(heads, 1)
        for h in range(NH + 1):
            for t in range(20 if h < NH else 16):
                if h or t >= 8:
                    quarter(5 * h + t // 4, t % 4)
                if h and t % 2 and t <= 11:
                    level(h - 1, (t + 3) // 2)
                if h and t == 12:
                    keys_to_tokens(h - 1)
                if h and t == 13:
                    key_values(h - 1)
                if h and t == 15:
                    outputs(h - 1)
                if h and t == 16:
                    output_stat(h - 1)
                if h and t == 17:
                    output_spread(h - 1)
                if h < NH and t == 17:
                    diagonal(h)
                if h < NH and t == 18:
                    token_major(5 * h + 3)
                if h < NH and t == 19:
                    level(h, 1)
                if h == NH and t >= 5 and t % 4 == 1:
                    token_major(5 * NH + (t - 5) // 4)
        output_stat(NH - 1)
        token_major(5 * NH + 3)

        pe.wait_ge(sem("dft_in"), 16 * 9)
        pe.wait_ge(sem("t_free"), 5 * NH + 3 + 2)
        pe.wait_ge(sem("o_std"), NH)

        def pos_dft(g):
            if g >= 2:
                pe.wait_ge(sem("v_re"), g - 1)
                pe.wait_ge(sem("v_im"), g - 1)
            pr = g % 2
            mm(PP[pr][:, 0, 0:P], UT[g][:, 0, :], DFTS[:, 256:384], start=True, stop=True)
            mm(PP[pr][:, 0, P:2 * P], UT[g][:, 0, :], DFTS[:, 384:512], start=True, stop=True)
            for part, out in ((0, PP[pr][:, 1, :]), (1, PP[2][:, g % 2, :])):
                for a in range(4):
                    m = mm(out, UT[g][:, 1 + a, :], DFTL[part][a][:, :], start=a == 0, stop=a == 3)
            m.then_inc(sem("v_ready"), 1)

        def ch_dft(g):
            pe.wait_ge(sem("v_re"), g + 1)
            pe.wait_ge(sem("v_im"), g + 1)
            if g:
                pe.wait_ge(sem("ylo_done"), g)
            for half in range(2):
                cols = slice(half * HALF, (half + 1) * HALF)
                mm(PP[3][:, half, 0:HALF], DFTS[:, 0:P], VRI[g][:, 0, cols], start=True, stop=False)
                m = mm(PP[3][:, half, 0:HALF], DFTS[:, P:2 * P], VRI[g][:, 1, cols], start=False, stop=True)
            m.then_inc(sem("yf_ready"), 1)

        pos_dft(0)
        output_spread(NH - 1)
        pe.wait_ge(sem("t_free"), 5 * NH + 4 + 2)
        pos_dft(1)
        pe.wait_ge(sem("o_full"), NH)
        ch_dft(0)
        pos_dft(2)
        ch_dft(1)
        pos_dft(3)
        ch_dft(2)
        ch_dft(3)

        ph = PLAN["mix_merge"]
        fh = [(Yhi[:, k, :], Ylo[:, k, :]) for k in range(NH)] + [(Ohi[:, k, :], Olo[:, k, :]) for k in range(NH)]
        with pe.Fori(0, ph.bodies) as j:
            for n2 in range(2):
                pe.wait_ge(sem("ga_ready"), j * 2 + (n2 + 1))
                slab(ph, j, 3 * n2, h_tiles, [0] * KT)
                pe.wait_ge(sem("gb_ready"), j * 2 + (n2 + 1))
                slab(ph, j, 3 * n2 + 1, h_tiles, [1] * KT)
                pe.wait_ge(sem("ylo_done"), NH)
                pe.wait_ge(sem("o_done"), NH)
                pe.wait_ge(sem("branch_b"), j * 2 + (n2 + 1))
                slab(ph, j, 3 * n2 + 2, fh, [2] * NH + [3] * NH)
        ph = PLAN["mix_out"]
        mg = [(MGhi[:, k, :], MGlo[:, k, :]) for k in range(KT)]
        pe.wait_ge(sem("ga_ready"), KT + 1)
        pe.wait_ge(sem("gb_ready"), KT + 1)
        slab(ph, 0, 0, mg, [0] * KT, ready=("mg_done", 1))
        slab(ph, 0, 1, mg, [1] * KT)
        with pe.Fori(1, ph.bodies) as j:
            for s in range(2):
                pe.wait_ge(sem("y_sq"), j * 2 + (KT + s + 1))
                slab(ph, j, s, mg, [s] * KT)
        boundary(1, KT)
        ffn_in(1)
        ffn_out(1, 2 * KT)
        boundary(2, 2 * KT, last=True)

    @block.scalar
    def _(act):
        A = nc.scalar.activation

        def rms(pr, features=D):
            return A(RQ[:, :], PP[pr][:, 0, 0:QT], ACT.Sqrt, bias=EPS, scale=float(D // features))

        def split_hi(ph, body, pos):
            act.wait_ge(raw_full[pos % 2], ph.raw_need(body, pos + 2))
            A(Whi[pos % 2][:, :, :], raw[pos % 2][:, :, :], ACT.Copy).then_inc(hi_done, 1)

        def slab_wait(ph, body, pos):
            act.wait_ge(slab_done, ph.slab(body, pos) + 1)

        act.wait_ge(sem("vec_T"), 2)
        act.wait_ge(sem("s2_zero"), 1)
        A(VA[:, :], PP[2][:, 0, 0:120], ACT.Copy).then_inc(sem("vec_evac"), 1)
        A(VB[:, :], PP[2][:, 1, 0:36], ACT.Copy).then_inc(sem("vec_evac"), 1)
        A(TT[2][:, 1:2], PP[2][:, 0, 0:1], ACT.Copy).then_inc(sem("gate_ready"), 1)
        A(TT[2][:, 2:3], PP[2][:, 0, 0:1], ACT.Copy).then_inc(sem("mid_hi"), 1)
        A(TT[2][:, 3:4], PP[2][:, 0, 0:1], ACT.Copy).then_inc(sem("ga_ready"), 1)
        A(TT[2][:, 4:5], PP[2][:, 0, 0:1], ACT.Copy).then_inc(sem("gb_ready"), 1)
        A(TT[2][:, 5:6], PP[2][:, 0, 0:1], ACT.Copy).then_inc(sem("y_sq"), 2)
        A(S2[:, :, 30], PP[2][:, 1, 28:36], ACT.Silu).then_inc(sem("silu_c"), 1)
        A(S2[:, :, 31], PP[2][:, 1, 20:28], ACT.Silu).then_inc(sem("silu_c"), 1)
        act.wait_ge(sem("lb_max"), 1)
        A(LB[:, 1:3, :], LB[:, 1:3, :], ACT.Exp).then_inc(sem("lb_exp"), 1)
        for n in range(KT):
            act.wait_ge(sem("x_T"), n + 1)
            A(XT[:, n, :], flat(n % 2)[:, 0:T], ACT.Copy)
            if n >= 2:
                act.wait_ge(sem("x_stat"), n - 1)
            A(TT[n % 2][:, :], flat(n % 2)[:, 0:T], ACT.Square).then_inc(sem("x_sq"), 1)
        act.wait_ge(sem("x_stat"), KT)
        rms(2).then_inc(sem("x_std"), 1)

        def mod_rows(slabs, rows):
            act.wait_ge(sem("mod_mm"), slabs)
            A(rows[:, :], PP[3][:, 0, :], ACT.Copy).then_inc(sem("modrow"), 1)

        mod_rows(MOD_EARLY, modrow)
        ph = PLAN["ffn0_in"]
        for s in range(2):
            act.wait_ge(raw_full[s], 16)
            A(Whi[s][:, :, :], raw[s][:, :, :], ACT.Copy).then_inc(hi_done, 1)

        def make_h(b):
            if b:
                act.wait_ge(sem("x_stat"), (b + 1) * KT)
                rms(2).then_inc(sem("x_std"), 1)
            else:
                act.wait_ge(sem("mod_set"), 1)

            def full(n):
                act.wait_ge(sem("h_scaled"), b * KT + n + 1)
                if n >= 3:
                    act.wait_ge(sem("h_ready"), b * KT + n - 2)
                for cond, t0, t1 in TOK:
                    m = A(BH[n % 3][:, t0:t1], BT[n % 3][:, t0:t1], ACT.Identity,
                          bias=MV[:, 3 * b * KT + n, cond:cond + 1], scale=Avec[:, b, n, cond:cond + 1])
                m.then_inc(sem("h_full"), 1)

            full(0)
            for n in range(KT):
                if 0 < n < KT - 1:
                    full(n + 1)
                act.wait_ge(sem("h_full"), b * KT + n + 1)
                A(Hhi[:, n, :], BH[n % 3][:, :], ACT.Copy).then_inc(sem("h_hi"), 1)
                if n == 0:
                    full(1)

        def boundary(b, last=False):
            act.wait_ge(sem("y_stat"), b + 1)
            rms(3).then_inc(sem("y_std"), 1)
            for n in range(KT):
                if last:
                    act.wait_ge(sem("out_T"), n + 1)
                    A(OUTB[:, :, n * P:(n + 1) * P], flat(n % 2)[:, 0:T].rearrange("p (a b) -> p a b", a=NCH),
                      ACT.Copy).then_inc(sem("out_tile"), 1)
                else:
                    act.wait_ge(*x_new_need(b, n))
                    if n >= 2:
                        act.wait_ge(sem("x_stat"), (b + 1) * KT + n - 1)
                    A(TT[n % 2][:, :], XT[:, n, :], ACT.Square).then_inc(sem("x_sq"), 1)

        def ffn_in(f):
            ph = PLAN[f"ffn{f}_in"]

            def step(j):
                slab_wait(ph, j, 0)
                split_hi(ph, j, 0)
                act.wait_ge(sem("hid_ready"), j + (f * FT + 1))
                A(two(TT[0][:, :]), halves(0), ACT.Silu).then_inc(sem("gate_ready"), 1)
                slab_wait(ph, j, 1)
                split_hi(ph, j, 1)
                act.wait_ge(sem("hid_ready"), j + (f * FT + 2))
                A(Mhi[:, bass.ds(j, 1), :], TT[1][:, :].rearrange("p (a b) -> p a b", a=1), ACT.Copy)\
                    .then_inc(sem("mid_hi"), 1)

            if f == 0:
                with act.Fori(0, MOD_LATE) as j:
                    step(j)
                mod_rows(MOD_EARLY + MOD_LATE, modrowl)
                with act.Fori(MOD_LATE, FT) as j:
                    step(j)
            else:
                with act.Fori(0, FT) as j:
                    step(j)

        def evac_y(j, n2, y0):
            b = y0 // KT
            act.wait_ge(sem("acc_done"), j * 2 + (y0 + n2 + 1))
            n = j * 2 + n2
            A(two(TT[n2][:, :]), halves(n2), ACT.Square).then_inc(sem("y_square"), 1)
            for cond, half, c0, c1 in ((0, 0, 0, CTX), (1, 0, CTX, HALF), (1, 1, 0, HALF)):
                m = A(Y[:, bass.ds(n, 1), half * HALF + c0:half * HALF + c1], PP[n2][:, half:half + 1, c0:c1],
                      ACT.Copy, scale=Gvec[:, b, bass.ds(n, 1), cond])
            m.then_inc(sem("y_sq"), 1)

        def ffn_out(f, y0, last=False):
            ph = PLAN[f"ffn{f}_out"]
            bodies = ph.bodies - 1 if last else ph.bodies
            act.wait_ge(sem("mod_set"), 2)
            with act.Fori(0, bodies) as j:
                for n2 in range(2):
                    for s in range(3):
                        slab_wait(ph, j, 3 * n2 + s)
                        split_hi(ph, j, 3 * n2 + s)
                    evac_y(j, n2, y0)
            if last:
                for n2 in range(2):
                    for s in range(3):
                        slab_wait(ph, bodies, 3 * n2 + s)
                        if 3 * n2 + s < 4:
                            split_hi(ph, bodies, 3 * n2 + s)
                    evac_y(bodies, n2, y0)

        make_h(0)
        ffn_in(0)
        ffn_out(0, 0)
        boundary(0)
        make_h(1)
        act.wait_ge(sem("h_ready"), 2 * KT)
        act.dma_start(maskf[:, :, :], t_mask).then_inc(sem("mask_in"), 16)

        def fourier_re(g):
            act.wait_ge(sem("v_ready"), g + 1)
            pr = g % 2
            A(VRI[g][:, :, 0:P], PP[pr][:, 0, 0:2 * P].rearrange("p (a b) -> p a b", a=2), ACT.Copy)
            A(VRI[g][:, 0, P:T], PP[pr][:, 1, :], ACT.Copy).then_inc(sem("v_re"), 1)

        def fourier_hi(g):
            act.wait_ge(sem("yf_ready"), g + 1)
            A(two(Yhi[:, g, :]), halves(3), ACT.Copy).then_inc(sem("yhi_done"), 1)

        heads = PLAN["mix_heads"]

        def evac_slab(i):
            s = i % 2
            act.wait_ge(slab_done, heads.base + i + 1)
            if i < 2:
                split_hi(heads, 0, i)
            act.wait_ge(sem("t_free"), i + 1)
            func = ACT.Copy if i >= 5 * NH or i % 5 == 3 else ACT.Sigmoid
            A(two(TT[s][:, :]), halves(s), func).then_inc(sem("t_ready"), 1)
            if i >= 2:
                split_hi(heads, 0, i)

        def level_keys(hd, lev):
            if lev == 1:
                act.wait_ge(sem("ks_ready"), hd + 1)
                if hd:
                    act.wait_ge(sem("lev_mm"), 8 * hd)
            else:
                act.wait_ge(sem("upd_done"), 8 * hd + lev)
                act.wait_ge(sem("lev_mm"), 8 * hd + lev - 1)
            h = 1 << (lev - 1)
            A(KX[lev % 2][:, :].rearrange("p (b e c) -> p b e c", e=2, c=h), level_ap(KD, hd, 0, T, h),
              ACT.Copy).then_inc(sem("kx_ready"), 1)

        def load_states(hd):
            for d in range(2):
                act.dma_start(SV[:, d, 0, :], state_hgrn[0, 0, d, hd]).then_inc(sem("state_in"), 16)

        def token_keys(hd):
            act.wait_ge(sem("kT"), hd + 1)
            for bank in range(2):
                m = A(KTOK[:, 4 * bank:4 * bank + 4, :],
                      PP[pair_of(hd, 0)][:, bank, :].rearrange("p (a b) -> p a b", a=4), ACT.Copy)
            m.then_inc(sem("ktok"), 1)

        def context_states(hd):
            act.wait_ge(sem("kv_mm"), hd + 1)
            if hd:
                act.wait_ge(sem("state_out"), 32 * hd)
            pr = pair_of(hd, 1)
            A(SO[:, :, :], PP[pr][:, :, 0:P], ACT.Copy).then_inc(sem("so_ready"), 1)
            act.wait_ge(sem("so_ready"), hd + 1)
            for d in range(2):
                act.dma_start(new_state[0, 0, d, hd], SO[:, d, :]).then_inc(sem("state_out"), 16)

        def output_square(hd):
            act.wait_ge(sem("o_mm"), hd + 1)
            A(OSQ[:, :], flat(pair_of(hd, 0))[:, 0:T], ACT.Square).then_inc(sem("o_sq"), 1)
            if hd + 1 < NH:
                load_states(hd + 1)

        def output_std(hd):
            act.wait_ge(sem("o_stat"), hd + 1)
            rms(pair_of(hd, 1), P).then_inc(sem("o_std"), 1)

        def output_hi(hd):
            act.wait_ge(sem("o_full"), hd + 1)
            A(Ohi[:, hd, :], OT[:, :], ACT.Copy).then_inc(sem("o_hi"), 1)

        load_states(0)
        for h in range(NH + 1):
            if h == NH - 1:
                act.wait_ge(sem("o_done"), 2)
                act.dma_start(DFTS[:, :], t_dft[:, 0:512]).then_inc(sem("dft_in"), 16)
                for part in range(2):
                    for a in range(4):
                        at = 512 + part * 2048 + a * 512
                        act.dma_start(DFTL[part][a][:, :], t_dft[:, at:at + 512]).then_inc(sem("dft_in"), 16)
            if h:
                level_keys(h - 1, 3)
            evac_slab(5 * h)
            if h:
                level_keys(h - 1, 4)
                level_keys(h - 1, 5)
            evac_slab(5 * h + 1)
            if h:
                level_keys(h - 1, 6)
                level_keys(h - 1, 7)
            evac_slab(5 * h + 2)
            if h:
                token_keys(h - 1)
                context_states(h - 1)
            if h < NH:
                level_keys(h, 1)
            evac_slab(5 * h + 3)
            if h:
                output_square(h - 1)
                output_std(h - 1)
            if h < NH:
                act.wait_ge(sem("lev_mm"), 8 * h + 1)
                A(AT[:, :], flat(pair_of(h, 0))[:, 0:T], ACT.Copy).then_inc(sem("at_start"), 1)
            if h:
                output_hi(h - 1)
            if h < NH:
                evac_slab(5 * h + 4)
                level_keys(h, 2)
        act.wait_ge(sem("o_done"), NH)
        for g in range(NH):
            fourier_re(g)
            if g >= 1:
                fourier_hi(g - 1)
        fourier_hi(NH - 1)

        ph = PLAN["mix_merge"]
        with act.Fori(0, ph.bodies) as j:
            for n2 in range(2):
                slab_wait(ph, j, 3 * n2)
                act.wait_ge(sem("mg_ready"), j * 2 + (n2 + 1))
                A(two(TT[0][:, :]), halves(0), ACT.Sigmoid).then_inc(sem("ga_ready"), 1)
                split_hi(ph, j, 3 * n2)
                slab_wait(ph, j, 3 * n2 + 1)
                A(two(TT[1][:, :]), halves(1), ACT.Sigmoid).then_inc(sem("gb_ready"), 1)
                split_hi(ph, j, 3 * n2 + 1)
                slab_wait(ph, j, 3 * n2 + 2)
                split_hi(ph, j, 3 * n2 + 2)
                act.wait_ge(sem("mg_ready"), j * 2 + (n2 + 2))
                A(MGhi[:, bass.ds(j * 2 + n2, 1), :], TT[2][:, :].rearrange("p (a b) -> p a b", a=1), ACT.Copy)\
                    .then_inc(sem("mg_hi"), 1)
        ph = PLAN["mix_out"]
        with act.Fori(0, ph.bodies) as j:
            for s in range(2):
                slab_wait(ph, j, s)
                split_hi(ph, j, s)
                evac_y(j, s, KT)
        boundary(1)
        make_h(2)
        ffn_in(1)
        ffn_out(1, 2 * KT, last=True)
        boundary(2, last=True)

    @block.vector
    def _(dve):
        V = nc.vector

        chain = [0]

        def link(ins):
            chain[0] += 1
            ins.then_inc(sem("dve_chain"), 1)
            dve.wait_ge(sem("dve_chain"), chain[0])

        V.memset(S2[:, :, :], 0.0).then_inc(sem("s2_zero"), 1)
        V.memset(ones_d[:, :], 1.0 / D).then_inc(sem("ones_set"), 1)
        link(V.memset(SEL[:, :, :], 0.0))
        for q in range(4):
            m = V.memset(SEL[32 * q:32 * q + 32, q, :], 1.0 / 32)
        m.then_inc(sem("ones_set"), 1)
        V.memset(spare[:, 1:2], 0.0).then_inc(sem("hid_ready"), 1)
        V.memset(spare[:, 6:7], 0.0).then_inc(sem("mid_lo"), 1)
        V.memset(spare[:, 7:8], 0.0).then_inc(sem("mg_done"), 1)
        V.memset(spare[:, 2:3], 0.0).then_inc(sem("mg_ready"), 1)
        V.memset(spare[:, 3:4], 0.0).then_inc(sem("branch_b"), 1)
        V.memset(spare[:, 4:5], 0.0).then_inc(sem("t_free"), 2)
        V.memset(spare[:, 5:6], 0.0).then_inc(sem("acc_done"), 2)
        dve.wait_ge(sem("vec_evac"), 2)
        link(V.tensor_tensor(LB[:, 0, :], VB[:, 4:12], VB[:, 12:20], ALU.max))
        link(V.tensor_tensor(LB[:, 1, :], VB[:, 4:12], LB[:, 0, :], ALU.subtract))
        V.tensor_tensor(LB[:, 2, :], VB[:, 12:20], LB[:, 0, :], ALU.subtract).then_inc(sem("lb_max"), 1)
        dve.wait_ge(sem("lb_exp"), 1)
        link(V.tensor_tensor(LB[:, 0, :], LB[:, 1, :], LB[:, 2, :], ALU.add))
        link(V.reciprocal(LB[:, 2, :], LB[:, 0, :]))
        link(V.tensor_tensor(LB[:, 3, :], LB[:, 1, :], LB[:, 2, :], ALU.mult))
        link(V.tensor_scalar(LB[:, 4, :], LB[:, 3, :], -1.0, 1.0, ALU.mult, ALU.add))

        def mod_vectors(block_at, t0, slabs):
            for cond in range(2):
                sums = PP[3][:, 1, block_at:block_at + P].rearrange("p (q i c) -> p i q c", q=4, c=2)
                link(V.tensor_tensor(MV[:, t0:t0 + 4 * slabs, cond].rearrange("p (i q) -> p i q", q=4),
                                     sums[:, 0:slabs, :, cond],
                                     VA[:, t0:t0 + 4 * slabs].rearrange("p (i q) -> p i q", q=4), ALU.add))

        def gains(b, pre_part, post_part):
            for cond in range(2):
                sc = MV[:, (3 * b + 1) * KT:(3 * b + 2) * KT, cond]
                gt = MV[:, (3 * b + 2) * KT:(3 * b + 3) * KT, cond]
                pre = VA[:, 72 + b * KT:72 + (b + 1) * KT]
                post = VA[:, 96 + b * KT:96 + (b + 1) * KT]
                if pre_part:
                    link(V.scalar_tensor_tensor(Avec[:, b, :, cond], sc, 1.0, pre, ALU.add, ALU.mult))
                if post_part:
                    link(V.scalar_tensor_tensor(Gvec[:, b, :, cond], gt, 1.0 if b == 1 else 0.5, post,
                                                ALU.mult, ALU.mult))

        def make_h(b):
            dve.wait_ge(sem("x_std"), b + 1)
            V.reciprocal(RQ[:, :], RQ[:, :]).then_inc(sem("x_rstd"), 1)
            if b == 0:
                dve.wait_ge(sem("mod_fold"), 1)
                mod_vectors(0, 0, MOD_EARLY)
                gains(0, True, False)
                V.memset(spare[:, 0:1], 0.0).then_inc(sem("mod_set"), 1)

            dve.wait_ge(sem("x_spread"), b + 1)

            def scaled(n):
                if n >= 3:
                    dve.wait_ge(sem("h_full"), b * KT + n - 2)
                V.tensor_tensor(two(BT[n % 3][:, :]), two(XT[:, n, :]), halves(2), ALU.mult)\
                    .then_inc(sem("h_scaled"), 1)

            for n in range(3):
                scaled(n)
            for n in range(KT):
                dve.wait_ge(sem("h_hi"), b * KT + n + 1)
                V.tensor_tensor(Hlo[:, n, :], BH[n % 3][:, :], Hhi[:, n, :].bitcast(fp32), ALU.subtract)\
                    .then_inc(sem("h_ready"), 1)
                if n + 3 < KT:
                    scaled(n + 3)

        def boundary(b):
            dve.wait_ge(sem("y_std"), b + 1)
            V.reciprocal(RQ[:, :], RQ[:, :]).then_inc(sem("y_rstd"), 1)
            dve.wait_ge(sem("y_spread"), b + 1)
            dve.wait_ge(sem("y_sq"), (b + 1) * KT + 2)

            def scaled(n):
                if n >= 6:
                    dve.wait_ge(*x_new_need(b, n - 6))
                V.tensor_tensor(two(BT[n % 6][:, :]), two(Y[:, n, :]), halves(3), ALU.mult)\
                    .then_inc(sem("y_scaled"), 1)

            scaled(0)
            for n in range(KT):
                if n + 1 < KT:
                    scaled(n + 1)
                if n not in POOL_TILES:
                    dve.wait_ge(sem("y_scaled"), b * KT + n + 1)
                    V.tensor_tensor(XT[:, n, :], XT[:, n, :], BT[n % 6][:, :], ALU.add).then_inc(sem("x_new_dve"), 1)

        def ffn_in(f):
            ph = PLAN[f"ffn{f}_in"]

            def step(j):
                dve.wait_ge(slab_done, ph.slab(j, 1) + 1)
                dve.wait_ge(sem("gate_ready"), j + (f * FT + 2))
                dve.wait_ge(sem("mid_hi"), j + (f * FT + 1))
                dve.wait_ge(sem("mid_lo"), j + (f * FT + 1))
                V.tensor_tensor(two(TT[1][:, :]), two(TT[0][:, :]), halves(1), ALU.mult)\
                    .then_inc(sem("hid_ready"), 1)
                dve.wait_ge(sem("mid_hi"), j + (f * FT + 2))
                V.tensor_tensor(Mlo[:, bass.ds(j, 1), :], TT[1][:, :].rearrange("p (a b) -> p a b", a=1),
                                Mhi[:, bass.ds(j, 1), :].bitcast(fp32), ALU.subtract).then_inc(sem("mid_lo"), 1)

            if f == 0:
                def window(i, s):
                    V.tensor_copy(SW[s][:, :, :], S2[:, :, bass.ds(i * -2 + 30, 32)])\
                        .then_inc(sem("sw_set"), 1)

                dve.wait_ge(sem("silu_c"), 2)
                dve.wait_ge(sem("h_ready"), KT)
                for s in range(2):
                    window(s, s)
                with dve.Fori(0, MOD_LATE // 2) as jj:
                    for s in range(2):
                        step(jj * 2 + s)
                        dve.wait_ge(sem("mod_mm"), jj * 2 + (MOD_EARLY + s + 1))
                        window(jj * 2 + (s + 2), s)
                step(MOD_LATE)
                dve.wait_ge(sem("mod_fold"), 2)
                mod_vectors(P, 2 * KT, MOD_LATE)
                gains(0, False, True)
                gains(1, True, True)
                gains(2, True, True)
                V.memset(LB[:, 0, 0:1], 0.0).then_inc(sem("mod_set"), 1)
                with dve.Fori(MOD_LATE + 1, FT) as j:
                    step(j)
            else:
                with dve.Fori(0, FT) as j:
                    step(j)

        def acc(j, n2, y0):
            dve.wait_ge(sem("y_square"), j * 2 + (y0 + n2 + 1))
            dve.wait_ge(sem("acc_done"), j * 2 + (y0 + n2 + 2))
            V.tensor_tensor(TT[2][:, :], TT[2][:, :], TT[n2][:, :], ALU.add).then_inc(sem("acc_done"), 1)

        def ffn_out(f, y0, last=False):
            ph = PLAN[f"ffn{f}_out"]
            link(V.memset(TT[2][:, :], 0.0))
            bodies = ph.bodies - 1 if last else ph.bodies
            with dve.Fori(0, bodies) as j:
                for n2 in range(2):
                    acc(j, n2, y0)
            if last:
                for n2 in range(2):
                    acc(bodies, n2, y0)

        make_h(0)
        ffn_in(0)
        ffn_out(0, 0)
        boundary(0)
        make_h(1)

        def fourier_im(g):
            dve.wait_ge(sem("v_ready"), g + 1)
            V.tensor_copy(VRI[g][:, 1, P:T], PP[2][:, g % 2, :]).then_inc(sem("v_im"), 1)

        def fourier_lo(g):
            dve.wait_ge(sem("yhi_done"), g + 1)
            V.tensor_tensor(two(Ylo[:, g, :]), halves(3), two(Yhi[:, g, :]).bitcast(fp32), ALU.subtract)\
                .then_inc(sem("ylo_done"), 1)

        dve.wait_ge(sem("mask_in"), 16)
        V.tensor_copy(mask[:, :, :], maskf[:, :, :]).then_inc(sem("mask_set"), 1)
        dve.wait_ge(sem("mask_set"), 1)

        def blocks(tensor, hd, array, h, side):
            return tensor[:, array, hd, :].rearrange("p (b c) -> p b c", c=2 * h)[:, :, side * h:(side + 1) * h]

        def totals(hd, array, h, side):
            ap = blocks(FD, hd, array, h, side)[:, :, 0:1]
            return ap.to_broadcast([P, T // (2 * h), h]) if h > 1 else ap

        def gated(i, dst):
            dve.wait_ge(sem("t_ready"), i + 1)
            V.tensor_tensor(two(dst), two(TT[i % 2][:, :]), halves(i % 2), ALU.mult).then_inc(sem("t_free"), 1)

        def gate_and_keys(i, d):
            hd = i // 5
            dve.wait_ge(sem("t_ready"), i + 1)
            at = d * NH + hd
            link(V.tensor_scalar(FD[:, 1 - d, hd, :], TT[i % 2][:, :], LB[:, 4, at:at + 1], LB[:, 3, at:at + 1],
                                 ALU.mult, ALU.add))
            V.tensor_scalar(KD[:, d, hd, :], FD[:, 1 - d, hd, :], -1.0, 1.0, ALU.mult, ALU.add)\
                .then_inc(sem("t_free"), 1)
            dve.wait_ge(sem("t_free"), i + 3)

        def token_copy(i, dst):
            dve.wait_ge(sem("tok_T"), i // 5 + 1 if i < 5 * NH else i - 4 * NH + 1)
            V.tensor_copy(dst, flat(i % 2)[:, 0:T].rearrange("p (a b) -> p a b", a=NCH)).then_inc(sem("t_free"), 1)

        def update(hd, lev):
            h = 1 << (lev - 1)
            dve.wait_ge(sem("lev_mm"), 8 * hd + lev + 1)
            dve.wait_ge(sem("upd_done"), 8 * hd + lev)
            V.tensor_tensor(blocks(KD, hd, 0, h, 0), blocks(KD, hd, 0, h, 0), totals(hd, 1, h, 1), ALU.mult)
            V.tensor_tensor(blocks(KD, hd, 1, h, 1), blocks(KD, hd, 1, h, 1), totals(hd, 0, h, 0), ALU.mult)
            V.tensor_tensor(blocks(QD, hd, 0, h, 0), blocks(QD, hd, 0, h, 0), totals(hd, 0, h, 1), ALU.mult)
            link(V.tensor_tensor(blocks(QD, hd, 1, h, 1), blocks(QD, hd, 1, h, 1), totals(hd, 1, h, 0), ALU.mult))
            tot = FD[:, :, hd, :].rearrange("p d (b c) -> p d b c", c=2 * h)
            V.tensor_tensor(tot[:, :, :, 0], tot[:, :, :, 0], tot[:, :, :, h], ALU.mult)\
                .then_inc(sem("upd_done"), 1)
            if lev == 1:
                dve.wait_ge(sem("at_start"), hd + 1)
            else:
                dve.wait_ge(sem("at_done"), 7 * hd + lev - 1)
            V.copy_predicated(AT[:, :].rearrange("p (a b) -> p a b", a=NCH),
                              mask[:, lev - 1:lev, :].to_broadcast([P, NCH, P]),
                              flat(pair_of(hd, lev))[:, 0:T].rearrange("p (a b) -> p a b", a=NCH))\
                .then_inc(sem("at_done"), 1)

        def carry_states(hd):
            dve.wait_ge(sem("state_in"), 32 * (hd + 1))
            dve.wait_ge(sem("so_ready"), hd + 1)
            kv = flat(pair_of(hd, 1))
            for e in range(3):
                V.scalar_tensor_tensor(SV[:, 0, e + 1, :], SV[:, 0, e, :], FD[:, 1, hd, (e + 1) * P:(e + 1) * P + 1],
                                       kv[:, (e + 1) * P:(e + 2) * P], ALU.mult, ALU.add)
                m = V.scalar_tensor_tensor(SV[:, 1, e + 1, :], SV[:, 1, e, :],
                                           FD[:, 0, hd, (4 - e) * P:(4 - e) * P + 1],
                                           kv[:, (7 - e) * P:(8 - e) * P], ALU.mult, ALU.add)
                if e < 2:
                    link(m)
                else:
                    m.then_inc(sem("sv_done"), 1)

        def output_gated(hd):
            dve.wait_ge(sem("o_sq"), hd + 1)
            if hd:
                dve.wait_ge(sem("o_done"), hd)
            V.scalar_tensor_tensor(OT[:, :], flat(pair_of(hd, 0))[:, 0:T], VB[:, hd:hd + 1], GT[:, hd, :],
                                   ALU.mult, ALU.mult).then_inc(sem("o_gated"), 1)
            dve.wait_ge(sem("o_std"), hd + 1)
            V.reciprocal(RQ[:, :], RQ[:, :]).then_inc(sem("o_rstd"), 1)

        def output_norm(hd):
            dve.wait_ge(sem("o_spread"), hd + 1)
            dve.wait_ge(sem("o_gated"), hd + 1)
            V.tensor_tensor(two(OT[:, :]), two(OT[:, :]), halves(pair_of(hd, 0)), ALU.mult).then_inc(sem("o_full"), 1)

        def output_lo(hd):
            dve.wait_ge(sem("o_hi"), hd + 1)
            V.tensor_tensor(Olo[:, hd, :], OT[:, :], Ohi[:, hd, :].bitcast(fp32), ALU.subtract)\
                .then_inc(sem("o_done"), 1)

        for h in range(NH + 1):
            if h:
                update(h - 1, 1)
                gated(5 * h - 1, GT[:, h - 1, :])
                update(h - 1, 2)
                update(h - 1, 3)
            if h < NH:
                gated(5 * h, QD[:, 0, h, :])
            if h:
                update(h - 1, 4)
            if h == NH:
                token_copy(5 * NH, UT[0][:, :, :])
            if h:
                update(h - 1, 5)
            if h < NH:
                gate_and_keys(5 * h + 1, 0)
                link(V.tensor_tensor(QD[:, 1, h, :], QD[:, 0, h, :], FD[:, 1, h, :], ALU.mult))
            if h:
                update(h - 1, 6)
            if h == NH:
                token_copy(5 * NH + 1, UT[1][:, :, :])
            if h:
                update(h - 1, 7)
            if h < NH:
                gate_and_keys(5 * h + 2, 1)
                V.tensor_tensor(KX[0][:, :], KD[:, 0, h, :], KD[:, 1, h, :], ALU.add).then_inc(sem("ks_ready"), 1)
            if h:
                carry_states(h - 1)
            if h == NH:
                token_copy(5 * NH + 2, UT[2][:, :, :])
            if h:
                output_gated(h - 1)
                if h == NH:
                    token_copy(5 * NH + 3, UT[3][:, :, :])
                output_norm(h - 1)
            if h < NH:
                dve.wait_ge(sem("lev_mm"), 8 * h + 1)
                V.tensor_tensor(QD[:, 0, h, :], QD[:, 0, h, :], FD[:, 0, h, :], ALU.mult).then_inc(sem("upd_done"), 1)
            if h:
                output_lo(h - 1)
            if h < NH:
                token_copy(5 * h + 3, VT[:, :, h * P:(h + 1) * P])
        for g in range(NH):
            fourier_im(g)
            if g >= 1:
                fourier_lo(g - 1)
        fourier_lo(NH - 1)

        ph = PLAN["mix_merge"]
        with dve.Fori(0, ph.bodies) as j:
            for n2 in range(2):
                dve.wait_ge(slab_done, ph.slab(j, 3 * n2 + 2) + 1)
                dve.wait_ge(sem("gb_ready"), j * 2 + (n2 + 2))
                V.tensor_tensor(two(TT[0][:, :]), two(TT[0][:, :]), halves(2), ALU.mult).then_inc(sem("branch_a"), 1)
                V.tensor_tensor(two(TT[1][:, :]), two(TT[1][:, :]), halves(3), ALU.mult).then_inc(sem("branch_b"), 1)
                dve.wait_ge(sem("branch_a"), j * 2 + (n2 + 1))
                dve.wait_ge(sem("branch_b"), j * 2 + (n2 + 2))
                dve.wait_ge(sem("mg_done"), j * 2 + (n2 + 1))
                V.tensor_tensor(TT[2][:, :], TT[0][:, :], TT[1][:, :], ALU.add).then_inc(sem("mg_ready"), 1)
                dve.wait_ge(sem("mg_hi"), j * 2 + (n2 + 1))
                V.tensor_tensor(MGlo[:, bass.ds(j * 2 + n2, 1), :], TT[2][:, :].rearrange("p (a b) -> p a b", a=1),
                                MGhi[:, bass.ds(j * 2 + n2, 1), :].bitcast(fp32), ALU.subtract)\
                    .then_inc(sem("mg_done"), 1)
        ph = PLAN["mix_out"]
        dve.wait_ge(sem("mg_done"), KT + 1)
        link(V.memset(TT[2][:, :], 0.0))
        with dve.Fori(0, ph.bodies) as j:
            for s in range(2):
                acc(j, s, KT)
        dve.wait_ge(sem("state_out"), 32 * NH)
        boundary(1)
        make_h(2)
        ffn_in(1)
        ffn_out(1, 2 * KT, last=True)
        boundary(2)

    block_cm.__exit__(None, None, None)


_INS = ["x_prompt", "x_sample", "state_hgrn", "c", "c_ctx", "w_mod", "b_mod", "norm_pre", "norm_post", "ffn_w_in",
        "ffn_w_out", "w_in", "w_four", "hgrn_gain", "w_hgrn", "w_out", "lb_logits"]
_OUTS = [(1, 128, 1024), (1, 512, 1024), (1, 1, 2, 4, 128, 128)]


def _tables():
    import numpy as np

    n = np.arange(P)
    const = np.zeros((P, P + 32), np.float32)
    const[n, n] = 1.0
    const[n, P + n % 32] = 1.0
    turn = 2 * np.pi * (np.outer(n, n) % P) / P
    t = np.arange(LAT)
    row, col = t // 64, t % 64
    turn_lat = 2 * np.pi * ((8 * (row[:, None] * row[None, :] % 8) + col[:, None] * col[None, :] % 64) % 64) / 64
    lat = [f(turn_lat).reshape(4, P, LAT).transpose(1, 0, 2).reshape(P, 4 * LAT) / 256 for f in (np.cos, np.sin)]
    dft = np.concatenate([np.cos(turn), -np.sin(turn), np.cos(turn) / P, np.sin(turn) / P] + lat, axis=1)
    x = n[:, None] ^ n[None, :]
    mask = np.stack([(x >> k) == 1 for k in range(7)], axis=1)
    return {"t_const": const, "t_dft": dft.astype(np.float32), "t_mask": mask.astype(np.float32)}


def kernel(**inputs):
    import numpy as _np
    import concourse.bacc as _bacc
    from concourse import mybir as _mybir
    from concourse.bass_utils import run_bass_kernel_spmd as _run

    nc = _bacc.Bacc("TRN2", target_bir_lowering=False, num_devices=1)
    arrays, args = {}, []
    feed = [(name, _np.ascontiguousarray(inputs[name])) for name in _INS] + list(_tables().items())
    for name, a in feed:
        arrays[f"in_{name}"] = a
        args.append(nc.dram_tensor(f"in_{name}", a.shape, _mybir.dt.from_np(a.dtype), kind="ExternalInput").ap())
    for i, shape in enumerate(_OUTS):
        args.append(nc.dram_tensor(f"out_{i}", shape, _mybir.dt.float32, kind="ExternalOutput").ap())
    hybrid_step_kernel(nc, *args)
    r = _run(nc, [arrays], core_ids=[0])
    return tuple(r.results[0][f"out_{i}"] for i in range(len(_OUTS)))
```
